# Optimizing a Trainium2 kernel written in Bass

```python
import math
import jax, jax.numpy as jnp
from jax import lax
import numpy as np

D_MODEL = 2048
BATCH = 1
SEQ = 512
DEPTH = 1
DEC_BATCH = 8
DEC_SEQ = 8
PAST_LEN = 2048
PAGE_SIZE = 128

HEAD_DIM_A = 64
N_HEADS_A = D_MODEL // 128
N_KV_A = N_HEADS_A // 4
GROUP_A = N_HEADS_A // N_KV_A
WINDOW = 128
ATTN_BLOCK = 128
N_HEADS_R = 8
DK_R = D_MODEL // (4 * N_HEADS_R)
DV_R = 2 * DK_R
RET_CHUNK = 128
PEER_HEADS = 8
N_KEYS = 128
N_EXPERTS = N_KEYS * N_KEYS
PEER_TOPK = 16
D_KEY = 256
D_KEY_HALF = D_KEY // 2
PEER_BLOCK = 128
PLE_DIM = 256
ROPE_THETA = 10000.0
EPS = 1e-6
NEG_INF = -1e30

IN_SIZES = (N_HEADS_A * HEAD_DIM_A, N_KV_A * HEAD_DIM_A, N_KV_A * HEAD_DIM_A,
            N_HEADS_R * DK_R, N_HEADS_R * DK_R, N_HEADS_R * DV_R, N_HEADS_R * DV_R,
            D_MODEL, D_MODEL)
IN_COLS = sum(IN_SIZES)

kernel_name = "hybrid_swa_retention_peer_step"

def _rms_norm(x, g):
    xf = x.astype(jnp.float32)
    y = xf * lax.rsqrt(jnp.mean(xf * xf, axis=-1, keepdims=True) + EPS)
    return (y * g.astype(jnp.float32)).astype(x.dtype)

def _rope(x, pos):
    d = x.shape[-1]
    inv = ROPE_THETA ** (-jnp.arange(0, d, 2, dtype=jnp.float32) / d)
    ang = pos.astype(jnp.float32)[:, None] * inv[None, :]
    cos = jnp.cos(ang)[:, None, :]
    sin = jnp.sin(ang)[:, None, :]
    xf = x.astype(jnp.float32)
    x1, x2 = xf[..., : d // 2], xf[..., d // 2:]
    return jnp.concatenate([x1 * cos - x2 * sin, x2 * cos + x1 * sin], axis=-1).astype(x.dtype)

def _sink_window_attention(q, k, v, q_pos, k_pos, sinks):
    s = jnp.einsum('bnqkgd,bnskd->bnkgqs', q, k).astype(jnp.float32) * (q.shape[-1] ** -0.5)
    diff = q_pos[:, :, None] - k_pos[:, None, :]
    ok = (diff >= 0) & (diff <= WINDOW) & (k_pos[:, None, :] >= 0)
    s = jnp.where(ok[None, :, None, None], s, NEG_INF)
    sink = sinks.astype(jnp.float32)[None, None, :, :, None, None]
    m = jnp.maximum(s.max(axis=-1, keepdims=True), sink)
    e = jnp.exp(s - m)
    p = e / (e.sum(axis=-1, keepdims=True) + jnp.exp(sink - m))
    return jnp.einsum('bnkgqs,bnskd->bnqkgd', p.astype(v.dtype), v)

def _retention(q, k, v, s0):
    Bn, T, H, _ = q.shape
    dv = v.shape[-1]
    C = math.gcd(T, RET_CHUNK)
    NC = T // C
    log_g = jnp.log1p(-jnp.exp2(-5.0 - jnp.arange(H, dtype=jnp.float32)))
    i = jnp.arange(C, dtype=jnp.float32)
    diff = i[:, None] - i[None, :]
    intra = jnp.where(diff[None] >= 0, jnp.exp(jnp.maximum(diff, 0.0)[None] * log_g[:, None, None]), 0.0)
    cross = jnp.exp((i + 1.0)[:, None] * log_g[None, :])
    kdec = jnp.exp((C - 1.0 - i)[:, None] * log_g[None, :])
    cdec = jnp.exp(C * log_g)

    def to_chunks(a):
        return a.astype(jnp.float32).reshape(Bn, NC, C, H, a.shape[-1]).transpose(1, 0, 2, 3, 4)

    def step(s, qkv):
        qc, kc, vc = qkv
        att = jnp.einsum('bihd,bjhd->bhij', qc, kc) * intra[None]
        o = (jnp.einsum('bhij,bjhv->bihv', att, vc)
             + jnp.einsum('bihd,bhdv->bihv', qc, s) * cross[None, :, :, None])
        s = s * cdec[None, :, None, None] + jnp.einsum('bjhd,bjhv->bhdv', kc * kdec[None, :, :, None], vc)
        return s, o

    s_fin, o = lax.scan(step, s0.astype(jnp.float32), (to_chunks(q), to_chunks(k), to_chunks(v)))
    o = o.transpose(1, 0, 2, 3, 4).reshape(Bn, T, H, dv)
    return o, s_fin.astype(s0.dtype)

def _peer(h, w_query, sub_keys, u_tab, v_tab):
    T = h.shape[0]
    qry = (h @ w_query).reshape(T, PEER_HEADS, 2, D_KEY_HALF)
    sc = jnp.einsum('thpc,pnc->thpn', qry, sub_keys).astype(jnp.float32)
    top_s, top_i = lax.top_k(sc, PEER_TOPK)
    comb = (top_s[:, :, 0, :, None] + top_s[:, :, 1, None, :]).reshape(T, PEER_HEADS, PEER_TOPK * PEER_TOPK)
    cidx = (top_i[:, :, 0, :, None] * N_KEYS + top_i[:, :, 1, None, :]).reshape(T, PEER_HEADS, PEER_TOPK * PEER_TOPK)
    best_s, best_j = lax.top_k(comb, PEER_TOPK)
    eidx = jnp.take_along_axis(cidx, best_j, axis=-1)
    gate = jax.nn.softmax(best_s, axis=-1)
    nblk = -(-T // PEER_BLOCK)
    pad = nblk * PEER_BLOCK - T
    hp = jnp.pad(h, ((0, pad), (0, 0))).reshape(nblk, PEER_BLOCK, D_MODEL)
    ip = jnp.pad(eidx, ((0, pad), (0, 0), (0, 0))).reshape(nblk, PEER_BLOCK, PEER_HEADS, PEER_TOPK)
    gp = jnp.pad(gate, ((0, pad), (0, 0), (0, 0))).reshape(nblk, PEER_BLOCK, PEER_HEADS, PEER_TOPK)

    def blk(args):
        hb, ib, gb = args
        u = u_tab[ib]
        a = jnp.einsum('bd,bhkd->bhk', hb, u).astype(jnp.float32)
        a = jax.nn.gelu(a, approximate=False) * gb
        return jnp.einsum('bhk,bhkd->bd', a.astype(v_tab.dtype), v_tab[ib])

    out = lax.map(blk, (hp, ip, gp)).reshape(nblk * PEER_BLOCK, D_MODEL)[:T]
    return out.astype(h.dtype)

def _layer(x, pe, pos0, k_buf, v_buf, s0, ln1, w_in, sinks, ln_ret, w_br_a, w_br_r, w_o,
           ln2, w_query, sub_keys, peer_u, peer_v, ln_ple, w_ple_gate, w_ple_proj):
    Bn, T, _ = x.shape
    pos = pos0 + jnp.arange(T, dtype=jnp.int32)
    h = _rms_norm(x, ln1)
    offs = [sum(IN_SIZES[:j]) for j in range(1, len(IN_SIZES))]
    q_a, k_a, v_a, q_r, k_r, v_r, g_r, gate_a, gate_r = jnp.split(h @ w_in, offs, axis=-1)

    q_a = _rope(q_a.reshape(Bn, T, N_HEADS_A, HEAD_DIM_A), pos).reshape(Bn, T, N_KV_A, GROUP_A, HEAD_DIM_A)
    k_a = _rope(k_a.reshape(Bn, T, N_KV_A, HEAD_DIM_A), pos)
    v_a = v_a.reshape(Bn, T, N_KV_A, HEAD_DIM_A)
    if k_buf is None:
        NB = T // ATTN_BLOCK
        qb = q_a.reshape(Bn, NB, ATTN_BLOCK, N_KV_A, GROUP_A, HEAD_DIM_A)
        kb = k_a.reshape(Bn, NB, ATTN_BLOCK, N_KV_A, HEAD_DIM_A)
        vb = v_a.reshape(Bn, NB, ATTN_BLOCK, N_KV_A, HEAD_DIM_A)
        k_ctx = jnp.concatenate([jnp.concatenate([jnp.zeros_like(kb[:, :1]), kb[:, :-1]], axis=1), kb], axis=2)
        v_ctx = jnp.concatenate([jnp.concatenate([jnp.zeros_like(vb[:, :1]), vb[:, :-1]], axis=1), vb], axis=2)
        q_pos = pos.reshape(NB, ATTN_BLOCK)
        k_pos = q_pos[:, :1] - ATTN_BLOCK + jnp.arange(2 * ATTN_BLOCK, dtype=jnp.int32)[None, :]
        new_k, new_v = k_a[:, -WINDOW:], v_a[:, -WINDOW:]
    else:
        k_all = jnp.concatenate([k_buf.astype(k_a.dtype), k_a], axis=1)
        v_all = jnp.concatenate([v_buf.astype(v_a.dtype), v_a], axis=1)
        qb, k_ctx, v_ctx = q_a[:, None], k_all[:, None], v_all[:, None]
        q_pos = pos[None, :]
        k_pos = (pos0 - WINDOW + jnp.arange(WINDOW + T, dtype=jnp.int32))[None, :]
        new_k, new_v = k_all[:, -WINDOW:], v_all[:, -WINDOW:]
    o_a = _sink_window_attention(qb, k_ctx, v_ctx, q_pos, k_pos, sinks.reshape(N_KV_A, GROUP_A))
    br_a = o_a.reshape(Bn, T, N_HEADS_A * HEAD_DIM_A) @ w_br_a

    q_r = _rope(q_r.reshape(Bn, T, N_HEADS_R, DK_R), pos)
    k_r = _rope(k_r.reshape(Bn, T, N_HEADS_R, DK_R), pos) * (DK_R ** -0.5)
    v_r = v_r.reshape(Bn, T, N_HEADS_R, DV_R)
    o_r, s_new = _retention(q_r, k_r, v_r, s0)
    mu = o_r.mean(axis=-1, keepdims=True)
    var = jnp.mean((o_r - mu) ** 2, axis=-1, keepdims=True)
    o_r = (o_r - mu) * lax.rsqrt(var + EPS) * ln_ret.astype(jnp.float32).reshape(N_HEADS_R, DV_R)
    o_r = o_r.reshape(Bn, T, N_HEADS_R * DV_R).astype(x.dtype) * jax.nn.silu(g_r)
    br_r = o_r @ w_br_r

    x = x + (jax.nn.sigmoid(gate_a) * br_a + jax.nn.sigmoid(gate_r) * br_r) @ w_o
    h2 = _rms_norm(x, ln2)
    x = x + _peer(h2.reshape(Bn * T, D_MODEL), w_query, sub_keys, peer_u, peer_v).reshape(Bn, T, D_MODEL)
    x = x + jax.nn.sigmoid(_rms_norm(x, ln_ple) @ w_ple_gate) * (pe @ w_ple_proj)
    return x, new_k, new_v, s_new

def setup_inputs(seed: int = 0) -> dict:
    key = jax.random.key(seed)
    ks = jax.random.split(key, 24)
    f = jnp.float32
    nrm = lambda k, shape, s=1.0: jax.random.normal(k, shape, f) * s
    gain = lambda k, shape: 1.0 + 0.02 * jax.random.normal(k, shape, f)
    return {
        "x_prompt": nrm(ks[0], (BATCH, SEQ, D_MODEL)),
        "x_sample": nrm(ks[1], (DEC_BATCH, DEC_SEQ, D_MODEL)),
        "cache_k_win": nrm(ks[2], (DEPTH, DEC_BATCH, WINDOW, N_KV_A, HEAD_DIM_A)),
        "cache_v_win": nrm(ks[3], (DEPTH, DEC_BATCH, WINDOW, N_KV_A, HEAD_DIM_A)),
        "state_ret": nrm(ks[4], (DEPTH, DEC_BATCH, N_HEADS_R, DK_R, DV_R)),
        "p_prompt": nrm(ks[5], (DEPTH, BATCH, SEQ, PLE_DIM)),
        "p_sample": nrm(ks[6], (DEPTH, DEC_BATCH, DEC_SEQ, PLE_DIM)),
        "ln1": gain(ks[7], (DEPTH, D_MODEL)),
        "w_in": nrm(ks[8], (DEPTH, D_MODEL, IN_COLS), D_MODEL ** -0.5),
        "attn_sinks": nrm(ks[9], (DEPTH, N_HEADS_A), 0.5),
        "ln_ret": gain(ks[10], (DEPTH, N_HEADS_R * DV_R)),
        "w_branch_attn": nrm(ks[11], (DEPTH, N_HEADS_A * HEAD_DIM_A, D_MODEL), (N_HEADS_A * HEAD_DIM_A) ** -0.5),
        "w_branch_ret": nrm(ks[12], (DEPTH, N_HEADS_R * DV_R, D_MODEL), (N_HEADS_R * DV_R) ** -0.5),
        "w_out": nrm(ks[13], (DEPTH, D_MODEL, D_MODEL), D_MODEL ** -0.5),
        "ln2": gain(ks[14], (DEPTH, D_MODEL)),
        "w_peer_query": nrm(ks[15], (DEPTH, D_MODEL, PEER_HEADS * D_KEY), D_MODEL ** -0.5),
        "peer_sub_keys": nrm(ks[16], (DEPTH, 2, N_KEYS, D_KEY_HALF), D_KEY_HALF ** -0.5),
        "peer_u": nrm(ks[17], (DEPTH, N_EXPERTS, D_MODEL), D_MODEL ** -0.5),
        "peer_v": nrm(ks[18], (DEPTH, N_EXPERTS, D_MODEL), PEER_HEADS ** -0.5),
        "ln_ple": gain(ks[19], (DEPTH, D_MODEL)),
        "w_ple_gate": nrm(ks[20], (DEPTH, D_MODEL, D_MODEL), D_MODEL ** -0.5),
        "w_ple_proj": nrm(ks[21], (DEPTH, PLE_DIM, D_MODEL), PLE_DIM ** -0.5),
        "ln_final": gain(ks[22], (D_MODEL,)),
    }

def reference(x_prompt, x_sample, cache_k_win, cache_v_win, state_ret, p_prompt, p_sample,
              ln1, w_in, attn_sinks, ln_ret, w_branch_attn, w_branch_ret, w_out, ln2,
              w_peer_query, peer_sub_keys, peer_u, peer_v, ln_ple, w_ple_gate, w_ple_proj, ln_final):
    xp, xs = x_prompt, x_sample
    kp_l, vp_l, sp_l, ks_l, vs_l, ss_l = [], [], [], [], [], []
    for i in range(DEPTH):
        lw = (ln1[i], w_in[i], attn_sinks[i], ln_ret[i], w_branch_attn[i], w_branch_ret[i], w_out[i],
              ln2[i], w_peer_query[i], peer_sub_keys[i], peer_u[i], peer_v[i],
              ln_ple[i], w_ple_gate[i], w_ple_proj[i])
        s0 = jnp.zeros((xp.shape[0], N_HEADS_R, DK_R, DV_R), xp.dtype)
        xp, kp, vp, sp = _layer(xp, p_prompt[i], 0, None, None, s0, *lw)
        xs, kn, vn, sn = _layer(xs, p_sample[i], PAST_LEN, cache_k_win[i], cache_v_win[i], state_ret[i], *lw)
        kp_l.append(kp); vp_l.append(vp); sp_l.append(sp)
        ks_l.append(kn); vs_l.append(vn); ss_l.append(sn)
    y_prompt = _rms_norm(xp, ln_final)
    y_sample = _rms_norm(xs, ln_final)
    return (y_prompt, y_sample, jnp.stack(kp_l), jnp.stack(vp_l), jnp.stack(sp_l),
            jnp.stack(ks_l), jnp.stack(vs_l), jnp.stack(ss_l))


_drawn_inputs = setup_inputs


def setup_inputs(seed=0):
    import zlib

    import numpy as np

    out = dict(_drawn_inputs(seed))
    spreads = {}
    factors = {'attn_sinks': 31.979, 'ln_ret': 11.412, 'ln_ple': 200.0, 'ln_final': 22.543, 'ln2': 9.599}
    for name, (base, spread) in spreads.items():
        noise = np.random.default_rng([zlib.crc32(name.encode()), seed]).standard_normal(out[name].shape)
        drawn = base * np.exp(spread * noise) if base else spread * noise
        out[name] = __import__('jax').numpy.asarray(drawn.astype(out[name].dtype))
    for name, factor in factors.items():
        out[name] = (out[name] * factor).astype(out[name].dtype)
    return out
```

```python
from contextlib import ExitStack, contextmanager

import numpy as np
import concourse.bass as bass
from concourse import mybir

F32 = mybir.dt.float32
F32R = mybir.dt.float32r
U32 = mybir.dt.uint32
ALU = mybir.AluOpType
ACT = mybir.ActivationFunctionType
AX = mybir.AxisListType

P = 128
D = 2048
KD = D // P
NP_TOK, NB_S, NS_S = 512, 8, 8
T = NP_TOK + NB_S * NS_S
TH = T // 2
TT = 5
ROWS = [P] * 4 + [T - 4 * P]
HA, KVA, DA = 16, 4, 64
HR, DKR, DVR = 8, 64, 128
PH, NK, TOPK = 8, 128, 16
PAST = 2048
EPS = 1e-6

QA, KA, VA, QR, KR, VR = 0, 8, 10, 12, 16, 20
N_FEAT = 28
GR, GA, GB = 0, 8, 24
N_SPILL = 40

B_IN = 0
B_BR = B_IN + (N_FEAT + N_SPILL) * 2
B_O = B_BR + KD * 2
B_Q = B_O + KD * 2
B_U = B_Q + KD * 2
NCHUNK = NK
GRP = 4
NG = NCHUNK // GRP
B_PG = B_U + 2 * NCHUNK * 2
N_BLOCKS = B_PG + 36

A_IN, A_BR = 0, N_FEAT
A_O = A_BR + 2 * KD
A_Q = A_O + KD
A_V = A_Q + KD
A_PG = A_V + NG * KD
R_IN, R_U = 0, N_SPILL
R_PG = R_U + NCHUNK

GT = 48
NGT = T // GT
SCALE = DA ** -0.5


class Chain:

    def __init__(self, eng, sem):
        self.eng, self.sem, self.n, self.loops = eng, sem, 0, []

    def did(self, ins):
        ins.then_inc(self.sem, 1)
        self.n += 1

    def wait(self, back=0):
        v = self.n - back
        for reg, per in self.loops:
            v = reg * per + v
        self.eng.wait_ge(self.sem, v)

    @contextmanager
    def loop(self, count, per):
        with self.eng.Fori(0, count) as i:
            start = self.n
            self.loops.append((i, per))
            yield i
            self.loops.pop()
            assert self.n - start == per, (self.n - start, per)
        self.n = start + per * count


def at_step(base, loops, scale=1):
    v = base
    for reg, per in loops:
        v = reg * (per * scale) + v
    return v


def halves(ap):
    return ap.rearrange("p (a b) -> p a b", a=2)


def build(nc, d, o):
    ctx = ExitStack()
    with ctx:
        base = (nc.sbuf_base + 63) // 64 * 64
        limit = base + nc.sbuf_bytes_remaining - 64

        def at(name, shape, dt, offset):
            size = 4
            for s in shape[1:]:
                size *= s
            assert offset % 4 == 0 and base + offset + size <= limit, (name, offset, size, limit - base)
            return nc.alloc_sbuf_tensor_at(name, shape, dt, offset=base + offset)

        def run(start, *items):
            out = []
            for name, shape, dt in items:
                out.append(at(name, shape, dt, start))
                size = 4
                for s in shape[1:]:
                    size *= s
                start += (size + 31) // 32 * 32
            return out, start

        TB = T * 4
        (raw, whi, wlo), e = run(0, ("w_raw", [P, 2, 8, P], F32), ("w_hi", [P, 2, 8, P], F32R),
                                 ("w_lo", [P, 2, 8, P], F32R))
        (ones, ident, swap, iota, lns, ln_ret, sink_q, nsink_q, sink_r, nsink_r, sub_k, cdec, rms_m, rstd), e = run(
            e, ("ones", [P, P], F32), ("ident", [P, P], F32), ("swap", [P, P], F32), ("iota", [P, P], F32),
            ("lns", [P, 4, KD], F32), ("ln_ret_c", [P, HR], F32), ("sink_q", [P, 8, 2], F32),
            ("nsink_q", [P, 8, 2], F32), ("sink_r", [P, 1], F32), ("nsink_r", [P, 1], F32),
            ("sub_k", [P, 2, NK], F32), ("cdec", [P, 2, 4], F32), ("rms_m", [P, T], F32), ("rstd", [P, T], F32))
        rA = e
        rX = rA
        rM = rA + KD * TB
        rH = rA + 38 * TB
        rZ = rH + 32 * TB

        x = at("x", [P, KD, T], F32, rX)
        h_hi = at("h_hi", [P, KD, T], F32R, rH)
        h_lo = at("h_lo", [P, KD, T], F32R, rH + KD * TB)
        (sq, hf), _ = run(rZ, ("sq", [P, 2, T], F32), ("hf", [P, 2, T], F32))
        feat = at("feat", [P, N_FEAT, T], F32, rA)
        (cos_t, sin_t, spill), e = run(rA + N_FEAT * TB, ("cos_t", [P, T], F32), ("sin_t", [P, T], F32),
                                       ("spill", [P, 2, T], F32))
        (pT, att, s_prompt, qx, rot_c, rot_s, qs), _ = run(
            rA + (N_FEAT + 2) * TB, ("pT", [P, 2, 4, P], F32), ("att", [P, 2, 2, P], F32),
            ("s_prompt", [P, 4, P], F32), ("qx", [P, 2, P], F32), ("rot_c", [P, T], F32), ("rot_s", [P, T], F32), ("qs", [P, NB_S, 2, 4 * NS_S], F32))
        (v_tok, k_tok, vr_tok, o_a, o_r), _ = run(
            rH, ("v_tok", [P, TT, 256], F32), ("k_tok", [P, TT, HR, DKR], F32), ("vr_tok", [P, TT, HR, DVR], F32),
            ("o_a", [P, 8, T], F32), ("o_r", [P, HR, T], F32))
        (ck, cv, mask_p, mask_c, mask_n, cross, kdec, mkd, sm, mx, sums, esink, den), _ = run(
            rZ, ("ck", [P, 2, 2, P], F32), ("cv", [P, 2, 256], F32), ("mask_p", [P, 256], F32),
            ("mask_c", [P, P], F32), ("mask_n", [P, NB_S, 64], F32), ("cross", [P, 4, 192], F32),
            ("kdec", [P, HR], F32), ("mkd", [P, HR, NB_S], F32), ("sm", [P, 2, 2, 256], F32),
            ("mx", [P, 2, 4], F32), ("sums", [P, 2, 2], F32), ("esink", [P, 2, 2], F32), ("den", [P, 2, 4], F32))
        (s0, intra, intra_s, kb), _ = run(
            rA + VR * TB, ("s0", [P, 2, NB_S, P], F32), ("intra", [P, HR, P], F32),
            ("intra_s", [P, HR, 64], F32), ("kb", [P, 2, NB_S, DKR], F32))
        (gn_d, gn_sq, gn_g), _ = run(rZ, ("gn_d", [P, 2, T], F32), ("gn_sq", [P, T], F32), ("gn_g", [P, 2, T], F32))
        (oa_hi, oa_lo, or_hi, or_lo), e = run(rA, ("oa_hi", [P, 8, T], F32R), ("oa_lo", [P, 8, T], F32R),
                                              ("or_hi", [P, 8, T], F32R), ("or_lo", [P, 8, T], F32R))
        (g_ab,), _ = run(e, ("g_ab", [P, 2, 2, T], F32))
        (br_t,), _ = run(rZ, ("br_t", [P, 3, T], F32))
        (qf, work, tv, ti, wv, wi, comb, hot, bv, bi, bab, bf, gij, gmx), _ = run(
            rM, ("qf", [P, 2, T], F32), ("work", [P, TT, NK], F32), ("tv", [P, TT, 16, TOPK], F32),
            ("ti", [P, TT, 16, TOPK], F32), ("wv", [P, TT, TOPK], F32), ("wi", [P, TT, TOPK], U32),
            ("comb", [P, PH, 256], F32), ("hot", [P, P, TOPK], F32), ("bv", [P, PH, TOPK], F32), ("bi", [P, P], U32),
            ("bab", [P, 2, P], U32), ("bf", [P, 2, P], F32), ("gij", [P, 3, P], F32), ("gmx", [P, 2, PH], F32))
        (gij_t, oh_cur, oh_j, oh_i), _ = run(
            rZ, ("gij_t", [P, T, 3], F32), ("oh_cur", [P, 2, 4, 3], F32), ("oh_j", [P, 2, 4, P], F32),
            ("oh_i", [P, 2, 4, P], F32))
        g_st = at("g_st", [P, 2, NK, GT], F32, rM)
        (a_hi, a_lo, g_in, gl), _ = run(rM, ("a_hi", [P, 2, GRP, T], F32R), ("a_lo", [P, 2, GRP, T], F32R),
                                        ("g_in", [P, 2, NGT, 2, GT], F32), ("gl", [P, 2, T], F32))
        (af,), _ = run(rZ, ("af", [P, 2, T], F32))
        (p_hi, p_lo, proj, sg), _ = run(rM, ("p_hi", [P, 2, T], F32R), ("p_lo", [P, 2, T], F32R),
                                        ("proj", [P, KD, T], F32), ("sg", [P, 2, T], F32))
        p_raw = at("p_raw", [P, 2, T], F32, rZ + 4 * TB)
        PS = ctx.enter_context(nc.psum_tensor("PS", [P, 8, 512], F32))

        def ring_a(t):
            return PS[:, 2 * (t % 2):2 * (t % 2) + 2, 0:TH]

        def ring_b(t):
            return PS[:, 4 + 2 * (t % 2):6 + 2 * (t % 2), 0:TH]

        names = """raw0 raw1 hi lo used free_a free_b vt const tab x x2 kv0 kv1 s0a s0b gn0 gn1 gab0 gab1 gin0 gin1
            p p_done spill0 spill1 gput0 gput1 out win_out kv_out sp_out chain passed passed_pe passed_act
            sq sqm ms rt h_done rot rotf rope tr_a tr_k tr_v trf_a trf_k trf_v
            as_mm as_m as_e as_p as_t as_tc as_o as_of bs_mm bs_m bs_e bs_p bs_t bs_tc bs_o bs_of
            rt_mm rt_at rt_qx rt_o rt_of rt_s rt_sf ro_c st_mm st_at st_kb st_o st_of st_s st_sf
            gn_mu gn_dd gn_q gn_v gn_vv gn_rt gn_done
            oab m_done sc_mm sc_f ft_x ft_e ft_g tr_g trf_g oh g_mm g_ev gl a_rdy pas""".split()
        S = {n: ctx.enter_context(nc.semaphore("s_" + n)) for n in names}
        s_raw = [S["raw0"], S["raw1"]]
        s_hi, s_lo, s_used, s_free_a, s_free_b = S["hi"], S["lo"], S["used"], S["free_a"], S["free_b"]
        block = ctx.enter_context(nc.Block())

        @block.sync
        def _(sp):
            def loads(b0, b1):
                with sp.Fori(0, (b1 - b0) // 2) as i:
                    for u in range(2):
                        sp.wait_ge(s_lo, i * 2 + (b0 + u - 1))
                        sp.dma_start(raw[:, u].rearrange("p m c -> p (m c)"), d["w"][i * 2 + (b0 + u)]
                                     ).then_inc(s_raw[u], 16)

            for u in range(2):
                sp.dma_start(raw[:, u].rearrange("p m c -> p (m c)"), d["w"][u]).then_inc(s_raw[u], 16)
            loads(2, B_U + 2)
            for tb in range(NGT):
                sp.wait_ge(S["g_ev"], 12 * (tb + 1) + 2)
                sp.dma_start(d["g_scr"][tb], g_st[:, tb % 2]).then_inc(S[f"gput{tb % 2}"], 16)
            loads(B_U + 2, N_BLOCKS)
            for n in range(KD // 2):
                sp.wait_ge(S["h_done"], 3 * KD + 2 * n + 2)
                sp.dma_start(o["y"][:, 2 * n:2 * n + 2], x[:, 2 * n:2 * n + 2]).then_inc(S["out"], 16)
            sp.wait_ge(S["out"], 16 * (KD // 2))
            sp.wait_ge(S["win_out"], 32)
            sp.wait_ge(S["kv_out"], 32)
            sp.wait_ge(S["sp_out"], 16)
            for u in range(2):
                sp.wait_ge(S[f"spill{u}"], 16 * (N_SPILL // 2))
                sp.wait_ge(S[f"gput{u}"], 16 * (NGT // 2))
                sp.wait_ge(S["s0a" if u == 0 else "s0b"], 64)

        @block.gpsimd
        def _(pool):
            const, tab, out = S["const"], S["tab"], S["win_out"]
            pool.dma_start(x[:], d["xT"]).then_inc(S["x"], 16)
            for dst, name in ((ones, "ones"), (ident, "ident"), (swap, "swap"), (iota, "iota"), (lns, "lns"),
                              (ln_ret, "ln_ret"), (sink_q, "sink_q"), (sink_r, "sink_r"), (sub_k, "sub_k"),
                              (cdec, "cdec")):
                pool.dma_start(dst[:], d[name]).then_inc(const, 16)
            pool.dma_start(o["kc"], d["cache_k"][:, NS_S:]).then_inc(out, 16)
            pool.dma_start(o["vc"], d["cache_v"][:, NS_S:]).then_inc(out, 16)
            with pool.Fori(0, N_SPILL // 2) as i:
                for u in range(2):
                    pool.wait_ge(s_free_b, i * 2 + (u + 1))
                    pool.dma_start(d["spill"][i * 2 + u], spill[:, u]).then_inc(S[f"spill{u}"], 16)
            pool.wait_ge(s_used, B_BR)
            for dst, name in ((cos_t, "cos"), (sin_t, "sin"), (mask_p, "mask_p"), (mask_c, "mask_c"),
                              (mask_n, "mask_n"), (cross, "cross"), (kdec, "kdec"), (mkd, "mkd")):
                pool.dma_start(dst[:], d[name]).then_inc(tab, 16)
            for b in range(2):
                pool.dma_start(ck[:, b], d["ckT"][:, b]).then_inc(S[f"kv{b}"], 16)
                pool.dma_start(cv[:, b], d["cache_v"][b]).then_inc(S[f"kv{b}"], 16)
            pool.wait_ge(S["rope"], 10)
            pool.dma_start(o["k_new"], feat[:, KA:KA + 2, 384:T]).then_inc(S["kv_out"], 16)
            pool.dma_start(o["v_new"], feat[:, VA:VA + 2, 384:T]).then_inc(S["kv_out"], 16)
            pool.wait_ge(S["tr_v"], TT)
            pool.dma_start(intra[:], d["intra"]).then_inc(tab, 16)
            pool.dma_start(intra_s[:], d["intra_s"]).then_inc(tab, 16)
            for t in range(2):
                pool.dma_start(s0[:, t], d["state"][:, t]).then_inc(S["s0a" if t == 0 else "s0b"], 16)
            for b in range(2, NB_S):
                pool.wait_ge(S["bs_o"], b - 1)
                pool.dma_start(ck[:, b % 2], d["ckT"][:, b]).then_inc(S[f"kv{b % 2}"], 16)
                pool.dma_start(cv[:, b % 2], d["cache_v"][b]).then_inc(S[f"kv{b % 2}"], 16)
            pool.wait_ge(S["rt_sf"], 16)
            pool.dma_start(o["s_pr"], s_prompt[:]).then_inc(S["sp_out"], 16)
            for t in range(4):
                pool.wait_ge(S["st_sf"], 2 * t + 2)
                sem = S["s0a" if t % 2 == 0 else "s0b"]
                pool.dma_start(o["s_smp"][:, t], s0[:, t % 2]).then_inc(sem, 16)
                if t < 2:
                    pool.wait_ge(sem, 32)
                    pool.dma_start(s0[:, t % 2], d["state"][:, t + 2]).then_inc(sem, 16)
            for u in range(2):
                pool.wait_ge(S[f"spill{u}"], 16 * (N_SPILL // 2))
            pool.wait_ge(S["gn_dd"], 1)
            for h in range(HR):
                if h >= 2:
                    pool.wait_ge(S["gn_done"], h - 1)
                pool.dma_start(gn_g[:, h % 2], d["spill"][GR + h]).then_inc(S[f"gn{h % 2}"], 16)
            pool.wait_ge(S["oab"], 8)
            pool.wait_ge(S["sp_out"], 16)
            for u in range(2):
                for r in range(2):
                    pool.dma_start(g_ab[:, u, r], d["spill"][u + (GA if r == 0 else GB)]).then_inc(S[f"gab{u}"], 16)
            with pool.Fori(1, KD // 2) as i:
                for u in range(2):
                    pool.wait_ge(S["m_done"], i * 2 + (u - 1))
                    for r in range(2):
                        pool.dma_start(g_ab[:, u, r], d["spill"][i * 2 + (u + (GA if r == 0 else GB))]
                                       ).then_inc(S[f"gab{u}"], 16)
            pool.wait_ge(s_used, B_O)
            pool.dma_start(x[:], d["xT"]).then_inc(S["x2"], 16)
            for u in range(2):
                pool.wait_ge(S[f"gput{u}"], 16 * (NGT // 2))
            for u in range(2):
                pool.dma_start(g_in[:, u], d["g_scr"][:, :, 2 * u:2 * u + 2].rearrange("b j i t -> j b i t")
                               ).then_inc(S[f"gin{u}"], 16)
            with pool.Fori(1, NCHUNK // 4) as i:
                for u in range(2):
                    pool.wait_ge(S["gl"], i * 4 + 2 * u)
                    pool.dma_start(g_in[:, u], d["g_scr"][:, :, bass.ds(i * 4 + 2 * u, 2)].rearrange(
                        "b j i t -> j b i t")).then_inc(S[f"gin{u}"], 16)
            pool.wait_ge(s_used, B_PG)
            pool.dma_start(p_raw[:], d["pT"]).then_inc(S["p"], 16)

        @block.scalar
        def _(act):
            def split(b, loops=()):
                act.wait_ge(s_raw[b % 2], at_step(16 * (b // 2 + 1), loops, 8))
                if b >= 2:
                    act.wait_ge(s_used, at_step(b - 1, loops))
                nc.scalar.activation(whi[:, b % 2], raw[:, b % 2], ACT.Copy).then_inc(s_hi, 1)

            def norm(r):
                with act.Fori(0, KD // 2) as i:
                    for u in range(2):
                        act.wait_ge(S["sqm"], i * 2 + (KD * r + u + 1))
                        nc.scalar.activation(sq[:, u], x[:, i * 2 + u], ACT.Square).then_inc(S["sq"], 1)
                act.wait_ge(S["ms"], r + 1)
                nc.scalar.activation(rstd[:], rms_m[:], ACT.Sqrt).then_inc(S["rt"], 1)

            split(0)
            act.wait_ge(S["x"], 16)
            norm(0)
            split(1)
            with act.Fori(0, N_FEAT) as i:
                split(2, [(i, 2)])
                split(3, [(i, 2)])

            def spilled(n, t0, func):
                def one(t, loops=()):
                    b = 2 * (N_FEAT + t)
                    split(b + 2, [(r, 4) for r in loops])
                    split(b + 3, [(r, 4) for r in loops])
                    if t >= 2:
                        act.wait_ge(S[f"spill{t % 2}"], at_step(16 * (t // 2), [(r, 1) for r in loops], 16))
                    nc.scalar.activation(halves(spill[:, t % 2]), ring_b(t), func).then_inc(s_free_b, 1)

                one(t0)
                one(t0 + 1)
                with act.Fori(0, n // 2 - 1) as i:
                    one(t0 + 2, [i])
                    one(t0 + 3, [i])

            spilled(8, 0, ACT.Silu)
            spilled(32, 8, ACT.Sigmoid)

            act.wait_ge(S["const"], 160)
            nc.scalar.activation(nsink_q[:], sink_q[:], ACT.Copy, scale=-1.0).then_inc(S["as_e"], 1)
            nc.scalar.activation(nsink_r[:], sink_r[:], ACT.Copy, scale=-1.0).then_inc(S["as_e"], 1)
            for tt in range(TT):
                n = ROWS[tt]
                act.wait_ge(S["tr_v"], tt + 1)
                nc.scalar.activation(vr_tok[0:n, tt].rearrange("p (a h) v -> p a (h v)", a=2), PS[0:n, 6:8, :],
                                     ACT.Copy).then_inc(S["trf_v"], 1)

            def exps(n):
                act.wait_ge(S["as_m"], n + 1)
                w = 128 if n % 4 == 0 else 256
                for u in range(2):
                    nc.scalar.activation(sm[:, n % 2, u, 0:w], sm[:, n % 2, u, 0:w], ACT.Exp,
                                         bias=mx[:, n % 2, 2 + u:3 + u],
                                         accum_out=sums[:, n % 2, u:u + 1]).then_inc(S["as_e"], 1)
                    nc.scalar.activation(esink[:, n % 2, u:u + 1], sink_q[:, n // 4, u:u + 1], ACT.Exp,
                                         bias=mx[:, n % 2, 2 + u:3 + u]).then_inc(S["as_e"], 1)

            def copy_pt(n):
                act.wait_ge(S["as_t"], n + 1)
                if n >= 2:
                    act.wait_ge(S["as_o"], n - 1)
                k = 2 if n % 4 == 0 else 4
                nc.scalar.activation(pT[:, n % 2, 0:k], PS[:, 4 + n % 2, 0:128 * k].rearrange(
                    "p (a b) -> p a b", b=P), ACT.Copy).then_inc(S["as_tc"], 1)

            for u in range(2):
                act.wait_ge(S[f"spill{u}"], 16 * (N_SPILL // 2))
            for n in range(32 + 1):
                if n < 32:
                    exps(n)
                if n >= 1:
                    copy_pt(n - 1)

            def exps_s(b):
                act.wait_ge(S["bs_m"], b + 1)
                nc.scalar.activation(sm[:, b % 2, 0, 0:192], sm[:, b % 2, 0, 0:192], ACT.Exp,
                                     bias=mx[:, b % 2, 1:2], accum_out=sums[:, b % 2, 0:1]).then_inc(S["bs_e"], 1)
                nc.scalar.activation(esink[:, b % 2, 0:1], sink_r[:], ACT.Exp,
                                     bias=mx[:, b % 2, 1:2]).then_inc(S["bs_e"], 1)

            def copy_pts(b):
                act.wait_ge(S["bs_t"], b + 1)
                if b >= 2:
                    act.wait_ge(S["bs_o"], b - 1)
                else:
                    act.wait_ge(S["as_o"], 32)
                nc.scalar.activation(pT[:, b % 2, 0], PS[:, 4 + b % 2, 0:P], ACT.Copy).then_inc(S["bs_tc"], 1)
                nc.scalar.activation(pT[0:64, b % 2, 1], PS[0:64, 4 + b % 2, P:2 * P], ACT.Copy
                                     ).then_inc(S["bs_tc"], 1)

            for b in range(NB_S + 1):
                if b < NB_S:
                    exps_s(b)
                if b >= 1:
                    copy_pts(b - 1)

            for n in range(16):
                c, t = n // 4, n % 4
                act.wait_ge(S["rt_o"], n + 1)
                nc.scalar.activation(o_r[:, 2 * t:2 * t + 2, c * P:(c + 1) * P], PS[:, 2:4, 0:P],
                                     ACT.Copy).then_inc(S["ro_c"], 1)
            for t in range(4):
                act.wait_ge(S["st_o"], t + 1)
                nc.scalar.activation(o_r[:, 2 * t:2 * t + 2, NP_TOK:T], PS[:, 2:4, 0:64],
                                     ACT.Copy).then_inc(S["ro_c"], 1)

            for h in range(HR):
                act.wait_ge(S["gn_dd"], h + 1)
                if h >= 1:
                    act.wait_ge(S["gn_v"], h)
                nc.scalar.activation(gn_sq[:], gn_d[:, h % 2], ACT.Square).then_inc(S["gn_q"], 1)
                act.wait_ge(S["gn_vv"], h + 1)
                nc.scalar.activation(rstd[:], rms_m[:], ACT.Sqrt).then_inc(S["gn_rt"], 1)

            def weights(b0, n, loops=()):
                with act.Fori(0, n) as j:
                    split(b0, [*loops, (j, 2)])
                    split(b0 + 1, [*loops, (j, 2)])

            weights(B_BR + 2, (B_Q - B_BR) // 2)
            act.wait_ge(s_free_a, A_Q)
            norm(1)
            weights(B_Q + 2, (B_U - B_Q) // 2)
            for tt in range(TT):
                act.wait_ge(S["ft_x"], tt + 1)
                nc.scalar.activation(bv[0:ROWS[tt]], bv[0:ROWS[tt]], ACT.Exp).then_inc(S["ft_e"], 1)
            act.sem_inc(S["g_ev"], 2)
            def spread(s, loops=()):
                with act.Fori(0, 6) as j:
                    for u in range(2):
                        act.wait_ge(S["g_mm"], at_step(12 * s + u + 3, [*loops, (j, 2)]))
                        nc.scalar.activation(
                            g_st[:, s % 2, :, bass.ds(j * 8 + 4 * u, 4)],
                            PS[:, 4 + u, :].rearrange("p (t i) -> p i t", t=4), ACT.Copy).then_inc(S["g_ev"], 1)

            spread(0)
            spread(1)
            with act.Fori(0, NGT // 2 - 1) as i:
                for s in range(2):
                    act.wait_ge(S[f"gput{s}"], i * 16 + 16)
                    act.sem_inc(S["passed_act"], 1)
                    spread(2 + s, [(i, 24)])

            def chunks(b0, t0, loops=()):
                with act.Fori(0, GRP // 2) as j:
                    for u in range(2):
                        bl = [*[(r, 16 * n) for r, n in loops], (j, 4)]
                        tl = [*[(r, GRP * n) for r, n in loops], (j, 2)]
                        split(b0 + 2 * u + 2, bl)
                        split(b0 + 2 * u + 3, bl)
                        act.wait_ge(S["gl"], at_step(t0 + u + 1, tl))
                        nc.scalar.activation(halves(gl[:, u]), ring_b(u), ACT.Gelu).then_inc(s_free_b, 1)

            chunks(B_U, 0)
            with act.Fori(0, NG // 2 - 1) as i:
                for g in range(2):
                    chunks(B_U + 8 + 16 * g, GRP * (g + 1), [(i, 2)])
                    weights(B_U + 18 + 16 * g, 4, [(i, 32)])
            chunks(B_PG - 24, GRP * (NG - 1))
            weights(B_PG - 14, 8)

            weights(B_PG + 2, 2)
            act.wait_ge(s_free_a, A_PG)
            norm(2)
            with act.Fori(0, KD // 2 - 1) as i:
                for u in range(2):
                    split(B_PG + 6 + 2 * u, [(i, 4)])
                    split(B_PG + 7 + 2 * u, [(i, 4)])
                    act.wait_ge(S["pas"], i * 2 + (u + 1))
                    nc.scalar.activation(halves(sg[:, u]), ring_b(u), ACT.Sigmoid).then_inc(s_free_b, 1)
            for n in (KD - 2, KD - 1):
                if n == KD - 2:
                    split(N_BLOCKS - 2)
                    split(N_BLOCKS - 1)
                act.wait_ge(s_used, B_PG + 4 + 2 * n + 2)
                act.wait_ge(S["pas"], n + 1)
                nc.scalar.activation(halves(sg[:, n % 2]), ring_b(n), ACT.Sigmoid).then_inc(s_free_b, 1)
            act.wait_ge(S["pas"], KD + 2)
            norm(3)

        @block.vector
        def _(dve):
            ch = Chain(dve, S["chain"])
            v = nc.vector

            def split(b, loops=()):
                dve.wait_ge(s_hi, at_step(b + 1, loops))
                v.tensor_tensor(wlo[:, b % 2], raw[:, b % 2], whi[:, b % 2].bitcast(F32), ALU.subtract
                                ).then_inc(s_lo, 1)

            def hi_lo(src, hi, lo):
                ch.did(v.tensor_copy(hi, src))
                ch.wait()
                return v.tensor_tensor(lo, src, hi.bitcast(F32), ALU.subtract)

            def inverse_root():
                ch.did(v.reciprocal(rstd[:], rstd[:]))
                ch.wait()
                ch.did(v.tensor_tensor(rms_m[:], rms_m[:], rstd[:], ALU.mult))
                ch.wait()
                ch.did(v.tensor_tensor(rms_m[:], rms_m[:], rstd[:], ALU.mult))
                ch.wait()
                ch.did(v.tensor_scalar(rms_m[:], rms_m[:], -0.5, 1.5, ALU.mult, ALU.add))
                ch.wait()
                ch.did(v.tensor_tensor(rstd[:], rstd[:], rms_m[:], ALU.mult))
                ch.wait()

            def norm(r, split_too):
                dve.wait_ge(S["sqm"], KD * (r + 1) + 2)
                v.tensor_scalar(halves(rms_m[:]), PS[:, 4:6, 0:TH], 1.0 / D, EPS, ALU.mult, ALU.add
                                ).then_inc(S["ms"], 1)
                dve.wait_ge(S["rt"], r + 1)
                inverse_root()
                if split_too:
                    with ch.loop(KD // 2, 4) as i:
                        for u in range(2):
                            ch.did(v.scalar_tensor_tensor(hf[:, u], x[:, i * 2 + u], lns[:, r, bass.ds(i * 2 + u, 1)],
                                                          rstd[:], ALU.mult, ALU.mult))
                            ch.wait()
                            hi_lo(hf[:, u], h_hi[:, i * 2 + u], h_lo[:, i * 2 + u]).then_inc(S["h_done"], 1)
                            dve.wait_ge(S["h_done"], i * 2 + (KD * r + u + 1))
                else:
                    with dve.Fori(0, KD // 2) as i:
                        for u in range(2):
                            v.scalar_tensor_tensor(x[:, i * 2 + u], x[:, i * 2 + u], lns[:, r, bass.ds(i * 2 + u, 1)],
                                                   rstd[:], ALU.mult, ALU.mult).then_inc(S["h_done"], 1)

            def weights(b0, n, loops=()):
                with dve.Fori(0, n) as j:
                    split(b0, [*loops, (j, 2)])
                    split(b0 + 1, [*loops, (j, 2)])

            split(0)
            dve.wait_ge(S["const"], 160)
            norm(0, True)
            split(1)
            with dve.Fori(0, N_FEAT // 2) as i:
                for u in range(2):
                    split(2 * u + 2, [(i, 4)])
                    split(2 * u + 3, [(i, 4)])
                    v.tensor_copy(halves(feat[:, i * 2 + u]), ring_a(u)).then_inc(s_free_a, 1)
            weights(2 * N_FEAT + 2, N_SPILL)
            dve.wait_ge(s_free_a, N_FEAT)

            dve.wait_ge(S["tab"], 16 * 8)
            ROPE = list(range(QA, KA + 2)) + list(range(QR, KR + 4))
            for r, f in enumerate(ROPE):
                s = DKR ** -0.5 if f >= KR else 1.0
                ch.did(v.scalar_tensor_tensor(rot_c[:], feat[:, f], s, cos_t[:], ALU.mult, ALU.mult))
                dve.wait_ge(S["rot"], r + 1)
                v.scalar_tensor_tensor(halves(rot_s[:]), PS[:, 2 * (r % 2):2 * (r % 2) + 2, 0:TH], s,
                                       halves(sin_t[:]), ALU.mult, ALU.mult).then_inc(S["rotf"], 1)
                ch.wait()
                dve.wait_ge(S["rotf"], r + 1)
                v.tensor_tensor(feat[:, f], rot_c[:], rot_s[:], ALU.add).then_inc(S["rope"], 1)
                dve.wait_ge(S["rope"], r + 1)
            for tt in range(TT):
                n = ROWS[tt]
                dve.wait_ge(S["tr_a"], tt + 1)
                v.tensor_copy(v_tok[0:n, tt], PS[0:n, 4, 0:256]).then_inc(S["trf_a"], 1)
                dve.wait_ge(S["tr_k"], tt + 1)
                src = PS[0:n, 5, :].rearrange("p (h k) -> p h k", h=HR)
                if tt < 4:
                    v.tensor_tensor(k_tok[0:n, tt], src, kdec[0:n, :].unsqueeze(2).broadcast_to([n, HR, DKR]),
                                    ALU.mult).then_inc(S["trf_k"], 1)
                else:
                    v.tensor_copy(k_tok[0:n, tt], src).then_inc(S["trf_k"], 1)

            def a_mask(n):
                w = 128 if n % 4 == 0 else 256
                q = n % 2
                dve.wait_ge(S["as_mm"], n + 1)
                if n >= 2:
                    dve.wait_ge(S["as_t"], n - 1)
                m = mask_p[:, 256 - w:256].unsqueeze(1).broadcast_to([P, 2, w])
                ch.did(v.scalar_tensor_tensor(sm[:, q, :, 0:w], PS[:, 2 * q:2 * q + 2, 0:w], SCALE, m,
                                              ALU.mult, ALU.add))
                ch.wait()
                ch.did(v.tensor_reduce(mx[:, q, 0:2], sm[:, q, :, 0:w], AX.X, ALU.max, negate=True))
                ch.wait()
                v.tensor_tensor(mx[:, q, 2:4], mx[:, q, 0:2], nsink_q[:, n // 4], ALU.min).then_inc(S["as_m"], 1)

            def a_prob(n):
                w = 128 if n % 4 == 0 else 256
                q = n % 2
                dve.wait_ge(S["as_e"], 4 * n + 6)
                ch.did(v.tensor_tensor(den[:, q, 0:2], sums[:, q], esink[:, q], ALU.add))
                ch.wait()
                ch.did(v.reciprocal(den[:, q, 2:4], den[:, q, 0:2]))
                ch.wait()
                v.tensor_tensor(sm[:, q, :, 0:w], sm[:, q, :, 0:w], den[:, q, 2:4].unsqueeze(2).broadcast_to([P, 2, w]),
                                ALU.mult).then_inc(S["as_p"], 1)

            def a_out(n):
                dve.wait_ge(S["as_o"], n + 1)
                v.tensor_copy(o_a[:, n // 4, (n % 4) * P:(n % 4 + 1) * P], PS[:, 6 + n % 2, 0:P]
                              ).then_inc(S["as_of"], 1)

            for p in range(2):
                ch.did(v.tensor_copy(qs[:, :, p].rearrange("p b (g s) -> p g b s", g=4),
                                     feat[:, QA + 4 * p:QA + 4 * p + 4, NP_TOK:T].rearrange(
                                         "p g (b s) -> p g b s", b=NB_S)))
            dve.wait_ge(S["as_e"], 2)
            for n in range(32 + 2):
                if n < 32:
                    a_mask(n)
                if 1 <= n < 33:
                    a_prob(n - 1)
                if n >= 2:
                    a_out(n - 2)

            def b_mask(b):
                q = b % 2
                dve.wait_ge(S["bs_mm"], b + 1)
                if b >= 2:
                    dve.wait_ge(S["bs_t"], b - 1)
                else:
                    dve.wait_ge(S["as_t"], 32)
                for kv in range(KVA):
                    r = slice(32 * kv, 32 * kv + 32)
                    bank = 2 * q + kv % 2
                    ch.did(v.scalar_tensor_tensor(sm[r, q, 0, 0:128], PS[r, bank, 0:128], SCALE, mask_c[r, :],
                                                  ALU.mult, ALU.add))
                    ch.did(v.scalar_tensor_tensor(sm[r, q, 0, 128:192], PS[r, bank, 128:192], SCALE,
                                                  mask_n[r, b], ALU.mult, ALU.add))
                ch.wait()
                ch.did(v.tensor_reduce(mx[:, q, 0:1], sm[:, q, 0, 0:192], AX.X, ALU.max, negate=True))
                ch.wait()
                v.tensor_tensor(mx[:, q, 1:2], mx[:, q, 0:1], nsink_r[:], ALU.min).then_inc(S["bs_m"], 1)

            def b_prob(b):
                q = b % 2
                dve.wait_ge(S["bs_e"], 2 * b + 2)
                ch.did(v.tensor_tensor(den[:, q, 0:1], sums[:, q, 0:1], esink[:, q, 0:1], ALU.add))
                ch.wait()
                ch.did(v.reciprocal(den[:, q, 1:2], den[:, q, 0:1]))
                ch.wait()
                v.tensor_scalar(sm[:, q, 0, 0:192], sm[:, q, 0, 0:192], den[:, q, 1:2], None, ALU.mult
                                ).then_inc(S["bs_p"], 1)

            def b_out(b):
                dve.wait_ge(S["bs_o"], b + 1)
                v.tensor_copy(o_a[:, :, NP_TOK + 8 * b:NP_TOK + 8 * b + 8],
                              PS[:, 6 + b % 2, 0:64].rearrange("p (g s) -> p g s", s=8)).then_inc(S["bs_of"], 1)

            for b in range(NB_S + 2):
                if b < NB_S:
                    b_mask(b)
                if 1 <= b < NB_S + 1:
                    b_prob(b - 1)
                if b >= 2:
                    b_out(b - 2)

            dve.wait_ge(S["tab"], 16 * 10)
            for n in range(16):
                c, t = n // 4, n % 4
                cols = slice(c * P, (c + 1) * P)
                if n >= 2:
                    dve.wait_ge(S["rt_o"], n - 1)
                v.tensor_tensor(qx[:, n % 2], feat[:, QR + t, cols], cross[:, t, 0:P], ALU.mult
                                ).then_inc(S["rt_qx"], 1)
                dve.wait_ge(S["rt_mm"], n + 1)
                v.tensor_tensor(att[:, n % 2], PS[:, 0:2, 0:P], intra[:, 2 * t:2 * t + 2], ALU.mult
                                ).then_inc(S["rt_at"], 1)
                dve.wait_ge(S["rt_s"], n + 1)
                if c == 0:
                    v.tensor_copy(s_prompt[:, t], PS[:, 6, 0:P]).then_inc(S["rt_sf"], 1)
                else:
                    dve.wait_ge(S["rt_sf"], n - 3)
                    v.scalar_tensor_tensor(s_prompt[:, t], s_prompt[:, t], cdec[:, 0, t:t + 1], PS[:, 6, 0:P],
                                           ALU.mult, ALU.add).then_inc(S["rt_sf"], 1)
                    dve.wait_ge(S["ro_c"], n + 1)
                    dst = o_r[:, 2 * t:2 * t + 2, cols]
                    v.tensor_tensor(dst, dst, PS[:, 4:6, 0:P], ALU.add).then_inc(S["rt_of"], 1)
            for t in range(4):
                if t < 2:
                    dve.wait_ge(S["rt_o"], 16)
                else:
                    dve.wait_ge(S["st_o"], t - 1)
                v.tensor_tensor(qx[:, t % 2, 0:64], feat[:, QR + t, NP_TOK:T], cross[:, t, P:P + 64], ALU.mult
                                ).then_inc(S["rt_qx"], 1)
                dve.wait_ge(S["st_mm"], t + 1)
                v.tensor_tensor(att[0:64, t % 2, :, 0:64], PS[0:64, 0:2, 0:64], intra_s[0:64, 2 * t:2 * t + 2],
                                ALU.mult).then_inc(S["st_at"], 1)
                if t:
                    dve.wait_ge(S["st_s"], 2 * t)
                for u in range(2):
                    h = 2 * t + u
                    v.tensor_tensor(kb[0:64, u], k_tok[0:64, 4, h].unsqueeze(1).broadcast_to([64, NB_S, DKR]),
                                    mkd[0:64, h].unsqueeze(2).broadcast_to([64, NB_S, DKR]), ALU.mult
                                    ).then_inc(S["st_kb"], 1)
                dve.wait_ge(S["ro_c"], 16 + t + 1)
                dst = o_r[:, 2 * t:2 * t + 2, NP_TOK:T]
                v.tensor_tensor(dst, dst, PS[:, 4:6, 0:64], ALU.add).then_inc(S["st_of"], 1)
                dve.wait_ge(S["s0a" if t % 2 == 0 else "s0b"], 16 * (1 + 2 * (t // 2)))
                for q in range(2):
                    dve.wait_ge(S["st_s"], 2 * t + q + 1)
                    st = s0[:, t % 2, 4 * q:4 * q + 4]
                    v.scalar_tensor_tensor(st, st, cdec[:, 1, t:t + 1],
                                           PS[:, 6 + q, :].rearrange("p (b v) -> p b v", b=4),
                                           ALU.mult, ALU.add).then_inc(S["st_sf"], 1)

            dve.wait_ge(S["st_sf"], 8)
            dve.wait_ge(S["st_of"], 4)
            dve.wait_ge(S["rt_of"], 12)
            dve.wait_ge(S["kv_out"], 32)
            for u in range(2):
                dve.wait_ge(S["s0a" if u == 0 else "s0b"], 64)
            for h in range(HR):
                dve.wait_ge(S["gn_mu"], h + 1)
                v.scalar_tensor_tensor(halves(gn_d[:, h % 2]), PS[:, 0:2, 0:TH], -1.0 / DVR, halves(o_r[:, h]),
                                       ALU.mult, ALU.add).then_inc(S["gn_dd"], 1)
                dve.wait_ge(S["gn_v"], h + 1)
                v.tensor_scalar(halves(rms_m[:]), PS[:, 2:4, 0:TH], 1.0 / DVR, EPS, ALU.mult, ALU.add
                                ).then_inc(S["gn_vv"], 1)
                dve.wait_ge(S["gn_rt"], h + 1)
                inverse_root()
                ch.did(v.scalar_tensor_tensor(gn_d[:, h % 2], gn_d[:, h % 2], ln_ret[:, h:h + 1], rstd[:],
                                              ALU.mult, ALU.mult))
                ch.wait()
                dve.wait_ge(S[f"gn{h % 2}"], 16 * (h // 2 + 1))
                ch.did(v.tensor_tensor(gn_d[:, h % 2], gn_d[:, h % 2], gn_g[:, h % 2], ALU.mult))
                ch.wait()
                hi_lo(gn_d[:, h % 2], or_hi[:, h], or_lo[:, h]).then_inc(S["gn_done"], 1)
                dve.wait_ge(S["gn_done"], h + 1)
            for t in range(8):
                hi_lo(o_a[:, t], oa_hi[:, t], oa_lo[:, t]).then_inc(S["oab"], 1)

            with ch.loop(KD // 2, 4) as i:
                for u in range(2):
                    dve.wait_ge(S[f"gab{u}"], i * 32 + 32)
                    for r in range(2):
                        b = B_BR + 2 * u + r
                        split(b + 2, [(i, 4)])
                        v.tensor_tensor(halves(br_t[:, r]), ring_a(r), halves(g_ab[:, u, r]), ALU.mult
                                        ).then_inc(s_free_a, 1)
                    dve.wait_ge(s_free_a, i * 4 + (A_BR + 2 * u + 2))
                    ch.did(v.tensor_tensor(br_t[:, 2], br_t[:, 0], br_t[:, 1], ALU.add))
                    ch.wait()
                    hi_lo(br_t[:, 2], h_hi[:, i * 2 + u], h_lo[:, i * 2 + u]).then_inc(S["m_done"], 1)
                    dve.wait_ge(S["m_done"], i * 2 + (u + 1))
            dve.wait_ge(S["x2"], 16)
            with dve.Fori(0, KD // 2) as i:
                for u in range(2):
                    split(B_O + 2 * u + 2, [(i, 4)])
                    split(B_O + 2 * u + 3, [(i, 4)])
                    xt = halves(x[:, i * 2 + u])
                    v.tensor_tensor(xt, xt, ring_a(u), ALU.add).then_inc(s_free_a, 1)
            dve.wait_ge(s_free_a, A_Q)
            norm(1, True)

            def query(t, loops=()):
                bl = [(r, 4) for r in loops]
                split(B_Q + 2 * t + 2, bl)
                split(B_Q + 2 * t + 3, bl)
                if t or loops:
                    dve.wait_ge(S["sc_mm"], at_step(t, [(r, 2) for r in loops]))
                v.tensor_copy(halves(qf[:, t % 2]), ring_a(t)).then_inc(s_free_a, 1)

            def settled():
                ch.wait()
                dve.sem_inc(S["passed"], 1)

            def top16(t, loops=()):
                dve.wait_ge(S["sc_mm"], at_step(t + 2, [(r, 2) for r in loops]))
                ch.did(v.tensor_copy(work[:, 0:4], PS[:, 6, :].rearrange("p (t n) -> p t n", t=4)))
                ch.did(v.tensor_copy(work[0:64, 4], PS[0:64, 7, 0:NK]))
                ch.wait()
                dve.sem_inc(S["sc_f"], 1)
                for k8 in (slice(0, 8), slice(8, 16)):
                    if k8.start:
                        for tt, n in enumerate(ROWS):
                            ch.did(v.match_replace(work[0:n, tt], wv[0:n, tt, 0:8], work[0:n, tt], -3.0e38))
                        settled()
                    for tt, n in enumerate(ROWS):
                        ch.did(v.max(wv[0:n, tt, k8], work[0:n, tt]))
                    settled()
                    for tt, n in enumerate(ROWS):
                        ch.did(v.max_index(wi[0:n, tt, k8], wv[0:n, tt, k8], work[0:n, tt]))
                    settled()
                tile = at_step(t, [(r, 2) for r in loops])
                ch.did(v.tensor_copy(tv[:, 0:4, tile], wv[:, 0:4]))
                ch.did(v.tensor_copy(ti[:, 0:4, tile], wi[:, 0:4]))
                ch.did(v.tensor_copy(tv[0:64, 4, tile], wv[0:64, 4]))
                ch.did(v.tensor_copy(ti[0:64, 4, tile], wi[0:64, 4]))
                ch.wait()

            dve.sem_inc(S["sc_f"], 1)
            query(0)
            with ch.loop(KD // 2 - 1, 2 * (2 + 5 * TT + 4)) as i:
                for u in range(2):
                    query(1 + u, [i])
                    top16(u, [i])
            query(KD - 1)
            top16(KD - 2)
            top16(KD - 1)

            for tt in range(TT):
                n = ROWS[tt]
                ch.wait()
                tvh = tv[0:n, tt].rearrange("p (h s) k -> p h s k", s=2)
                tih = ti[0:n, tt].rearrange("p (h s) k -> p h s k", s=2)
                for s_h in range(PH):
                    ch.did(v.tensor_tensor(comb[0:n, s_h].rearrange("p (a b) -> p a b", a=TOPK),
                                           tvh[:, s_h, 0].unsqueeze(2).broadcast_to([n, TOPK, TOPK]),
                                           tvh[:, s_h, 1].unsqueeze(1).broadcast_to([n, TOPK, TOPK]), ALU.add))
                if tt:
                    dve.wait_ge(S["tr_g"], tt)
                biv = bi[0:n].rearrange("p (h k) -> p h k", h=PH)
                for half in range(2):
                    k8 = slice(8 * half, 8 * half + 8)
                    ch.wait()
                    for h in range(PH):
                        ch.did(v.max(bv[0:n, h, k8], comb[0:n, h]))
                    ch.wait()
                    for h in range(PH):
                        ch.did(v.max_index(biv[:, h, k8], bv[0:n, h, k8], comb[0:n, h]))
                    if half == 0:
                        ch.wait()
                        for h in range(PH):
                            ch.did(v.match_replace(comb[0:n, h], bv[0:n, h, k8], comb[0:n, h], -3.0e38))
                ch.wait()
                ch.did(v.tensor_copy(gmx[0:n, 0], bv[0:n, :, 0]))
                ch.wait()
                v.tensor_tensor(bv[0:n], bv[0:n], gmx[0:n, 0].unsqueeze(2).broadcast_to([n, PH, TOPK]),
                                ALU.subtract).then_inc(S["ft_x"], 1)
                ch.did(v.tensor_scalar(bab[0:n, 0], bi[0:n], 4, None, ALU.logical_shift_right))
                ch.did(v.tensor_scalar(bab[0:n, 1], bi[0:n], 15, None, ALU.bitwise_and))
                ch.wait()
                ch.did(v.tensor_copy(bf[0:n], bab[0:n]))
                for s in range(2):
                    ch.wait()
                    ch.did(v.tensor_tensor(hot[0:n], bf[0:n, s].unsqueeze(2).broadcast_to([n, P, TOPK]),
                                           iota[0:n, 0:TOPK].unsqueeze(1).broadcast_to([n, P, TOPK]), ALU.is_equal))
                    ch.wait()
                    hot4 = hot[0:n].rearrange("p (h k) a -> p h k a", h=PH)
                    ch.did(v.tensor_tensor(hot4, hot4, tih[:, :, s].unsqueeze(2).broadcast_to([n, PH, TOPK, TOPK]),
                                           ALU.mult))
                    ch.wait()
                    ch.did(v.tensor_reduce(gij[0:n, 1 + s], hot[0:n], AX.X, ALU.add))
                dve.wait_ge(S["ft_e"], tt + 1)
                ch.did(v.tensor_reduce(gmx[0:n, 1], bv[0:n], AX.X, ALU.add))
                ch.wait()
                ch.did(v.reciprocal(gmx[0:n, 1], gmx[0:n, 1]))
                ch.wait()
                v.tensor_tensor(gij[0:n, 0].rearrange("p (h k) -> p h k", h=PH), bv[0:n],
                                gmx[0:n, 1].unsqueeze(2).broadcast_to([n, PH, TOPK]), ALU.mult
                                ).then_inc(S["ft_g"], 1)
                dve.wait_ge(S["tr_g"], tt + 1)
                v.tensor_copy(gij_t[:, tt * P:tt * P + n], PS[:, 0, 0:384].rearrange("p (c t) -> p t c", c=3)[:, 0:n]
                              ).then_inc(S["trf_g"], 1)
            dve.wait_ge(S["trf_g"], TT)

            with ch.loop(T // 8, 16) as i:
                for u in range(2):
                    dve.wait_ge(S["g_mm"], i * 2 + (u + 1))
                    ch.did(v.tensor_copy(oh_cur[:, u], gij_t[:, bass.ds(i * 8 + 4 * u, 4)]))
                    ch.wait()
                    for k in range(4):
                        ch.did(v.tensor_scalar(oh_j[:, u, k], iota[:], oh_cur[:, u, k, 2:3], None, ALU.is_equal))
                        last = v.tensor_scalar(oh_i[:, u, k], iota[:], oh_cur[:, u, k, 1:2], oh_cur[:, u, k, 0:1],
                                               ALU.is_equal, ALU.mult)
                        if k < 3:
                            ch.did(last)
                        else:
                            last.then_inc(S["oh"], 1)
                            dve.wait_ge(S["oh"], i * 2 + (u + 1))

            def chunks(par, b0, g0, loops=()):
                bl, tl = [(r, 16 * n) for r, n in loops], [(r, GRP * n) for r, n in loops]
                for c in range(GRP):
                    t = GRP * g0 + c
                    split(b0 + 2 * c + 2, bl)
                    split(b0 + 2 * c + 3, bl)
                    dve.wait_ge(s_free_b, at_step(N_SPILL + t + 1, tl))
                    if c % 2 == 0:
                        dve.wait_ge(S[f"gin{c // 2}"], at_step(16 * (g0 + 1), loops, 16))
                    v.tensor_tensor(af[:, c % 2].rearrange("p (a b) -> p a b", a=NGT),
                                    gl[:, c % 2].rearrange("p (a b) -> p a b", a=NGT), g_in[:, c // 2, :, c % 2],
                                    ALU.mult).then_inc(S["gl"], 1)
                    dve.wait_ge(S["gl"], at_step(t + 3, tl))
                    hi_lo(af[:, c % 2], a_hi[:, par, c], a_lo[:, par, c]).then_inc(S["a_rdy"], 1)
                    dve.wait_ge(S["a_rdy"], at_step(t + 1, tl))

            def values(b0, g0, loops=()):
                bl, tl = [(r, 16 * n) for r, n in loops], [(r, KD * n) for r, n in loops]
                vl = [(r, 8 * n) for r, n in loops]
                dve.wait_ge(s_free_a, at_step(A_V + KD * g0, tl))
                dve.sem_inc(S["passed"], 1)
                with dve.Fori(0, 4) as j:
                    for s in range(2):
                        dve.wait_ge(S["vt"], at_step(8 * g0 + s + 1, [*vl, (j, 2)]))
                        xt = halves(x[:, j * 4 + 2 * s])
                        v.tensor_tensor(xt, xt, ring_a(0), ALU.add).then_inc(s_free_a, 1)
                        split(b0 + s + 2, [*bl, (j, 2)])
                        xt = halves(x[:, j * 4 + (2 * s + 1)])
                        v.tensor_tensor(xt, xt, ring_a(1), ALU.add).then_inc(s_free_a, 1)

            dve.sem_inc(S["gl"], 2)
            chunks(0, B_U, 0)
            with ch.loop(NG // 2 - 1, 2 * GRP) as i:
                for g in range(2):
                    chunks((g + 1) % 2, B_U + 8 + 16 * g, g + 1, [(i, 2)])
                    values(B_U + 16 + 16 * g, g, [(i, 2)])
            chunks(1, B_PG - 24, NG - 1)
            values(B_PG - 16, NG - 2)
            values(B_PG - 8, NG - 1)
            dve.wait_ge(s_free_a, A_PG)

            dve.wait_ge(S["p"], 16)
            for k in range(2):
                hi_lo(p_raw[:, k], p_hi[:, k], p_lo[:, k]).then_inc(S["p_done"], 1)
            for q in range(4):
                for m in range(4):
                    if m < 3:
                        dve.wait_ge(S["vt"], 8 * NG + 3 * q + m + 1)
                    else:
                        dve.wait_ge(s_used, B_PG + q + 1)
                        split(B_PG + q + 2)
                    v.tensor_copy(halves(proj[:, 4 * q + m]), ring_a(m)).then_inc(s_free_a, 1)
            dve.wait_ge(s_free_a, A_PG + KD)
            norm(2, True)
            dve.sem_inc(S["pas"], 2)

            def ple(t, loops=(), more=True):
                bl, tl = [(r, 4) for r in loops], [(r, 2) for r in loops]
                if more:
                    split(B_PG + 4 + 2 * t + 2, bl)
                    split(B_PG + 4 + 2 * t + 3, bl)
                dve.wait_ge(s_free_b, at_step(N_SPILL + NCHUNK + t + 1, tl))
                n = at_step(t, tl)
                ch.did(v.tensor_tensor(proj[:, n], proj[:, n], sg[:, t % 2], ALU.mult))
                ch.wait()
                v.tensor_tensor(x[:, n], x[:, n], proj[:, n], ALU.add).then_inc(S["pas"], 1)

            with ch.loop(KD // 2 - 1, 2) as i:
                for u in range(2):
                    ple(u, [i])
            ple(KD - 2)
            ple(KD - 1, more=False)
            dve.wait_ge(S["pas"], KD + 2)
            norm(3, False)

        @block.tensor
        def _(pe):
            mm = nc.tensor.matmul

            def tile(dst, w, slot_k, xh, xl, ks, first, last):
                slot, m, kt = slot_k
                wh = whi[:, slot].rearrange("p (m k) c -> p m k c", k=kt)
                wl = wlo[:, slot].rearrange("p (m k) c -> p m k c", k=kt)
                for n, k in enumerate(ks):
                    for r, (w, xx) in enumerate(((wh, xh), (wh, xl), (wl, xh))):
                        for a in range(2):
                            ins = mm(dst[:, a], w[:, m, n], xx[:, k, a * TH:(a + 1) * TH],
                                     start=first and n == 0 and r == 0,
                                     stop=last and n == len(ks) - 1 and r == 2)
                return ins

            def full_tile(dst, b, xh, xl, loops=()):
                for s in range(2):
                    pe.wait_ge(s_lo, at_step(b + s + 1, loops))
                    tile(dst, None, ((b + s) % 2, 0, 8), xh, xl, range(8 * s, 8 * s + 8), s == 0, s == 1
                         ).then_inc(s_used, 1)

            def norm(r):
                for k in range(KD):
                    pe.wait_ge(S["sq"], KD * r + k + 1)
                    for a in range(2):
                        ins = mm(PS[:, 4 + a, 0:TH], ones[:], sq[:, k % 2, a * TH:(a + 1) * TH],
                                 start=k == 0, stop=k == KD - 1)
                    ins.then_inc(S["sqm"], 1)

            pe.wait_ge(S["const"], 160)
            pe.sem_inc(S["sqm"], 2)
            norm(0)
            pe.wait_ge(S["h_done"], KD)

            def project(ring, s_free, f0, t0, b0, n):
                for t in range(2):
                    if f0:
                        pe.wait_ge(s_free, f0 + t - 1)
                    full_tile(ring(t), b0 + 2 * t, h_hi, h_lo)
                with pe.Fori(1, n // 2) as i:
                    for u in range(2):
                        pe.wait_ge(s_free, i * 2 + (f0 + u - 1))
                        full_tile(ring(u), b0 + 2 * u, h_hi, h_lo, [(i, 4)])

            project(ring_a, s_free_a, 0, 0, B_IN, N_FEAT)
            project(ring_b, s_free_b, 0, 0, B_IN + 2 * N_FEAT, N_SPILL)

            ROPE = list(range(QA, KA + 2)) + list(range(QR, KR + 4))
            pe.wait_ge(s_free_a, A_BR)
            pe.wait_ge(s_free_b, N_SPILL)
            for r, f in enumerate(ROPE):
                if r >= 2:
                    pe.wait_ge(S["rotf"], r - 1)
                for a in range(2):
                    ins = mm(PS[:, 2 * (r % 2) + a, 0:TH], swap[:], feat[:, f, a * TH:(a + 1) * TH],
                             start=True, stop=True)
                ins.then_inc(S["rot"], 1)
            for tt in range(TT):
                n = ROWS[tt]
                c = slice(tt * P, tt * P + n)
                if tt:
                    pe.wait_ge(S["trf_a"], tt)
                for f in range(2):
                    ins = pe.transpose(PS[0:n, 4, f * P:(f + 1) * P], feat[:, VA + f, c], ident[:])
                ins.then_inc(S["tr_a"], 1)
                if tt:
                    pe.wait_ge(S["trf_v"], tt)
                for f in range(8):
                    ins = pe.transpose(PS[0:n, 6 + f // 4, (f % 4) * P:(f % 4 + 1) * P], feat[:, VR + f, c], ident[:])
                ins.then_inc(S["tr_v"], 1)
                if tt:
                    pe.wait_ge(S["trf_k"], tt)
                else:
                    pe.wait_ge(S["rope"], len(ROPE))
                for f in range(4):
                    ins = pe.transpose(PS[0:n, 5, f * P:(f + 1) * P], feat[:, KR + f, c], ident[:])
                ins.then_inc(S["tr_k"], 1)

            def a_scores(n):
                t, c = n // 4, n % 4
                if n >= 2:
                    pe.wait_ge(S["as_m"], n - 1)
                k0 = max(c - 1, 0) * P
                w = (c + 1) * P - k0
                for u in range(2):
                    r = slice(64 * u, 64 * u + 64)
                    ins = mm(PS[:, 2 * (n % 2) + u, 0:w], feat[r, QA + t, c * P:(c + 1) * P],
                             feat[r, KA + t // 4, k0:(c + 1) * P], start=True, stop=True)
                ins.then_inc(S["as_mm"], 1)

            def a_turn(n):
                pe.wait_ge(S["as_p"], n + 1)
                if n >= 2:
                    pe.wait_ge(S["as_tc"], n - 1)
                else:
                    pe.wait_ge(S["trf_a"], TT)
                    pe.wait_ge(S["trf_k"], TT)
                nb = 1 if n % 4 == 0 else 2
                for u in range(2):
                    for k in range(nb):
                        j = u * nb + k
                        ins = pe.transpose(PS[:, 4 + n % 2, j * P:(j + 1) * P], sm[:, n % 2, u, k * P:(k + 1) * P],
                                           ident[:])
                ins.then_inc(S["as_t"], 1)

            def a_values(n):
                t, c = n // 4, n % 4
                pe.wait_ge(S["as_tc"], n + 1)
                if n >= 2:
                    pe.wait_ge(S["as_of"], n - 1)
                else:
                    pe.wait_ge(S["trf_v"], TT)
                nb = 1 if c == 0 else 2
                for u in range(2):
                    kv = 2 * (t // 4) + u
                    for k in range(nb):
                        ins = mm(PS[64 * u:64 * u + 64, 6 + n % 2, 0:P],
                                 v_tok[:, c - nb + 1 + k, kv * DA:(kv + 1) * DA], pT[:, n % 2, u * nb + k],
                                 start=k == 0, stop=k == nb - 1)
                ins.then_inc(S["as_o"], 1)

            for n in range(32 + 2):
                if n < 32:
                    a_scores(n)
                if 1 <= n < 33:
                    a_turn(n - 1)
                if n >= 2:
                    a_values(n - 2)

            def b_scores(b):
                pe.wait_ge(S[f"kv{b % 2}"], 32 * (b // 2 + 1))
                if b >= 2:
                    pe.wait_ge(S["bs_m"], b - 1)
                else:
                    pe.wait_ge(S["as_m"], 32)
                for kv in range(KVA):
                    p, u = kv // 2, kv % 2
                    r = slice(64 * u, 64 * u + 64)
                    q = qs[r, b, p]
                    rows = slice(32 * kv, 32 * kv + 32)
                    bank = 2 * (b % 2) + u
                    mm(PS[rows, bank, 0:P], q, ck[r, b % 2, p], start=True, stop=True)
                    ins = mm(PS[rows, bank, P:P + 64], q, feat[r, KA + p, NP_TOK:T], start=True, stop=True)
                ins.then_inc(S["bs_mm"], 1)

            def b_turn(b):
                pe.wait_ge(S["bs_p"], b + 1)
                if b >= 2:
                    pe.wait_ge(S["bs_tc"], 2 * b - 2)
                else:
                    pe.wait_ge(S["as_tc"], 32)
                pe.transpose(PS[:, 4 + b % 2, 0:P], sm[:, b % 2, 0, 0:P], ident[:])
                pe.transpose(PS[0:64, 4 + b % 2, P:2 * P], sm[:, b % 2, 0, P:P + 64], ident[:]
                             ).then_inc(S["bs_t"], 1)

            def b_values(b):
                pe.wait_ge(S["bs_tc"], 2 * b + 2)
                if b >= 2:
                    pe.wait_ge(S["bs_of"], b - 1)
                else:
                    pe.wait_ge(S["as_of"], 32)
                for kv in range(KVA):
                    p, u = kv // 2, kv % 2
                    dst = PS[64 * u:64 * u + 64, 6 + b % 2, 32 * p:32 * p + 32]
                    c = slice(kv * DA, (kv + 1) * DA)
                    r = slice(32 * kv, 32 * kv + 32)
                    mm(dst, cv[:, b % 2, c], pT[:, b % 2, 0, r], start=True, stop=False)
                    ins = mm(dst, v_tok[0:64, 4, c], pT[0:64, b % 2, 1, r], start=False, stop=True)
                ins.then_inc(S["bs_o"], 1)

            for b in range(NB_S + 2):
                if b >= 2:
                    b_values(b - 2)
                if b < NB_S:
                    b_scores(b)
                if 1 <= b < NB_S + 1:
                    b_turn(b - 1)

            pe.wait_ge(S["bs_m"], NB_S)
            pe.wait_ge(S["bs_tc"], 2 * NB_S)
            pe.wait_ge(S["bs_of"], NB_S)
            for n in range(16):
                c, t = n // 4, n % 4
                cols = slice(c * P, (c + 1) * P)
                if n:
                    pe.wait_ge(S["rt_at"], n)
                for u in range(2):
                    r = slice(64 * u, 64 * u + 64)
                    ins = mm(PS[:, u, 0:P], feat[r, KR + t, cols], feat[r, QR + t, cols], start=True, stop=True)
                ins.then_inc(S["rt_mm"], 1)
                if c:
                    pe.wait_ge(S["rt_qx"], n + 1)
                    pe.wait_ge(S["rt_sf"], n - 3)
                    if n > 4:
                        pe.wait_ge(S["rt_of"], n - 4)
                    for u in range(2):
                        r = slice(64 * u, 64 * u + 64)
                        mm(PS[:, 4 + u, 0:P], s_prompt[r, t], qx[r, n % 2], start=True, stop=True)
                if n:
                    pe.wait_ge(S["rt_sf"], n)
                for u in range(2):
                    h = 2 * t + u
                    ins = mm(PS[64 * u:64 * u + 64, 6, 0:P], k_tok[:, c, h], vr_tok[:, c, h], start=True, stop=True)
                ins.then_inc(S["rt_s"], 1)
                pe.wait_ge(S["rt_at"], n + 1)
                if n:
                    pe.wait_ge(S["ro_c"], n)
                for u in range(2):
                    ins = mm(PS[:, 2 + u, 0:P], vr_tok[:, c, 2 * t + u], att[:, n % 2, u], start=True, stop=True)
                ins.then_inc(S["rt_o"], 1)
            pe.wait_ge(S["rt_of"], 12)
            for t in range(4):
                pe.wait_ge(S["st_at"] if t else S["rt_at"], t if t else 16)
                for u in range(2):
                    r = slice(64 * u, 64 * u + 64)
                    ins = mm(PS[0:64, u, 0:64], feat[r, KR + t, NP_TOK:T], feat[r, QR + t, NP_TOK:T],
                             start=True, stop=True)
                ins.then_inc(S["st_mm"], 1)
                pe.wait_ge(S["rt_qx"], 16 + t + 1)
                pe.wait_ge(S["s0a" if t % 2 == 0 else "s0b"], 16 * (1 + 2 * (t // 2)))
                if t:
                    pe.wait_ge(S["st_of"], t)
                for u in range(2):
                    r = slice(64 * u, 64 * u + 64)
                    for b in range(NB_S):
                        mm(PS[:, 4 + u, 8 * b:8 * b + 8], s0[r, t % 2, b], qx[r, t % 2, 8 * b:8 * b + 8],
                           start=True, stop=True)
                pe.wait_ge(S["st_kb"], 2 * t + 2)
                if t:
                    pe.wait_ge(S["st_sf"], 2 * t)
                else:
                    pe.wait_ge(S["rt_sf"], 16)
                for q in range(2):
                    for u in range(2):
                        for b in range(4):
                            ins = mm(PS[64 * u:64 * u + 64, 6 + q, b * P:(b + 1) * P], kb[0:64, u, 4 * q + b],
                                     vr_tok[0:64, 4, 2 * t + u], start=True, stop=True)
                    ins.then_inc(S["st_s"], 1)
                pe.wait_ge(S["st_at"], t + 1)
                pe.wait_ge(S["ro_c"], 16 + t)
                for u in range(2):
                    ins = mm(PS[:, 2 + u, 0:64], vr_tok[0:64, 4, 2 * t + u], att[0:64, t % 2, u, 0:64],
                             start=True, stop=True)
                ins.then_inc(S["st_o"], 1)

            pe.wait_ge(S["ro_c"], 20)
            pe.wait_ge(S["st_of"], 4)
            for h in range(HR):
                if h:
                    pe.wait_ge(S["gn_dd"], h)
                else:
                    pe.wait_ge(S["st_at"], 4)
                for a in range(2):
                    ins = mm(PS[:, a, 0:TH], ones[:], o_r[:, h, a * TH:(a + 1) * TH], start=True, stop=True)
                ins.then_inc(S["gn_mu"], 1)
                pe.wait_ge(S["gn_q"], h + 1)
                if h:
                    pe.wait_ge(S["gn_vv"], h)
                for a in range(2):
                    ins = mm(PS[:, 2 + a, 0:TH], ones[:], gn_sq[:, a * TH:(a + 1) * TH], start=True, stop=True)
                ins.then_inc(S["gn_v"], 1)

            pe.wait_ge(S["oab"], 8)
            pe.wait_ge(S["gn_vv"], HR)
            for m in range(2):
                for r, (xh, xl) in enumerate(((oa_hi, oa_lo), (or_hi, or_lo))):
                    b = B_BR + 2 * m + r
                    pe.wait_ge(s_free_a, A_BR + 2 * m + r - 1)
                    pe.wait_ge(s_lo, b + 1)
                    tile(ring_a(r), None, (r, 0, 8), xh, xl, range(8), True, True).then_inc(s_used, 1)
            with pe.Fori(2, KD) as m:
                for r, (xh, xl) in enumerate(((oa_hi, oa_lo), (or_hi, or_lo))):
                    pe.wait_ge(s_free_a, m * 2 + (A_BR + r - 1))
                    pe.wait_ge(s_lo, m * 2 + (B_BR + r + 1))
                    tile(ring_a(r), None, (r, 0, 8), xh, xl, range(8), True, True).then_inc(s_used, 1)
            pe.wait_ge(S["m_done"], KD)
            project(ring_a, s_free_a, A_O, 0, B_O, KD)
            norm(1)
            pe.wait_ge(S["h_done"], 2 * KD)

            def query(t, loops=()):
                pe.wait_ge(s_free_a, at_step(A_Q + t - 1, [(r, 2) for r in loops]))
                full_tile(ring_a(t), B_Q + 2 * t, h_hi, h_lo, [(r, 4) for r in loops])

            def scores(t, loops=()):
                l2 = [(r, 2) for r in loops]
                pe.wait_ge(s_free_a, at_step(A_Q + t + 1, l2))
                pe.wait_ge(S["sc_f"], at_step(t + 1, l2))
                for tt, n in enumerate(ROWS):
                    ins = mm(PS[0:n, 6 + tt // 4, (tt % 4) * NK:(tt % 4 + 1) * NK], qf[:, t % 2, tt * P:tt * P + n],
                             sub_k[:, t % 2], start=True, stop=True)
                ins.then_inc(S["sc_mm"], 1)

            pe.sem_inc(S["sc_mm"], 1)
            query(0)
            with pe.Fori(0, KD // 2 - 1) as i:
                for u in range(2):
                    query(1 + u, [i])
                    scores(u, [i])
            query(KD - 1)
            scores(KD - 2)
            scores(KD - 1)

            pe.wait_ge(s_free_a, A_V)
            for tt, n in enumerate(ROWS):
                pe.wait_ge(S["ft_g"], tt + 1)
                if tt:
                    pe.wait_ge(S["trf_g"], tt)
                for c in range(3):
                    ins = pe.transpose(PS[:, 0, c * P:c * P + n], gij[0:n, c], ident[0:n, 0:n])
                ins.then_inc(S["tr_g"], 1)
            pe.sem_inc(S["g_mm"], 2)
            with pe.Fori(0, T // 8) as i:
                for u in range(2):
                    pe.wait_ge(S["oh"], i * 2 + (u + 1))
                    pe.wait_ge(S["g_ev"], i * 2 + (u + 1))
                    for k in range(4):
                        ins = mm(PS[:, 4 + u, k * P:(k + 1) * P], oh_j[:, u, k], oh_i[:, u, k], start=True, stop=True)
                    ins.then_inc(S["g_mm"], 1)
            pe.wait_ge(S["g_ev"], T // 4 + 2)

            def chunks(b0, g0, loops=()):
                bl, tl = [(r, 16 * n) for r, n in loops], [(r, GRP * n) for r, n in loops]
                with pe.Fori(0, GRP // 2) as j:
                    for u in range(2):
                        pe.wait_ge(s_free_b, at_step(N_SPILL + GRP * g0 + u - 1, [*tl, (j, 2)]))
                        full_tile(ring_b(u), b0 + 2 * u, h_hi, h_lo, [*bl, (j, 4)])

            def values(par, b0, g0, loops=()):
                bl, tl = [(r, 16 * n) for r, n in loops], [(r, KD * n) for r, n in loops]
                pe.wait_ge(S["a_rdy"], at_step(GRP * (g0 + 1), [(r, GRP * n) for r, n in loops]))
                pe.sem_inc(S["passed_pe"], 1)
                with pe.Fori(0, 4) as j:
                    for s in range(2):
                        pe.wait_ge(s_lo, at_step(b0 + s + 1, [*bl, (j, 2)]))
                        for m in range(2):
                            pe.wait_ge(s_free_a, at_step(A_V + KD * g0 + 2 * s + m - 1, [*tl, (j, 4)]))
                            tile(ring_a(m), None, (s, m, GRP), a_hi[:, par], a_lo[:, par], range(GRP), True, True
                                 ).then_inc(S["vt"] if m == 0 else s_used, 1)

            chunks(B_U, 0)
            with pe.Fori(0, NG // 2 - 1) as i:
                for g in range(2):
                    chunks(B_U + 8 + 16 * g, g + 1, [(i, 2)])
                    values(g, B_U + 16 + 16 * g, g, [(i, 2)])
            chunks(B_PG - 24, NG - 1)
            values(0, B_PG - 16, NG - 2)
            values(1, B_PG - 8, NG - 1)

            pe.wait_ge(S["p_done"], 2)
            for q in range(4):
                pe.wait_ge(s_lo, B_PG + q + 1)
                for m in range(4):
                    pe.wait_ge(s_free_a, A_PG + 4 * q + m - 1)
                    tile(ring_a(m), None, (q % 2, m, 2), p_hi, p_lo, range(2), True, True
                         ).then_inc(S["vt"] if m < 3 else s_used, 1)
            norm(2)
            pe.wait_ge(S["h_done"], 3 * KD)
            project(ring_b, s_free_b, N_SPILL + NCHUNK, 0, B_PG + 4, KD)
            norm(3)


def _tables():
    f = np.float32
    t = {}
    t["ones"] = np.ones((P, P), f)
    t["ident"] = np.eye(P, dtype=f)
    sw = np.zeros((P, P), f)
    for p in range(P):
        if p % 64 < 32:
            sw[p + 32, p] = -1.0
        else:
            sw[p - 32, p] = 1.0
    t["swap"] = sw
    t["iota"] = np.tile(np.arange(P, dtype=f), (P, 1))
    inv = (f(10000.0) ** (-np.arange(0, DA, 2, dtype=f) / f(DA))).astype(f)
    pos = np.concatenate([np.arange(NP_TOK), PAST + np.tile(np.arange(NS_S), NB_S)]).astype(f)
    ang = (pos[None, :] * inv[:, None]).astype(f)
    t["cos"] = np.tile(np.cos(ang), (4, 1)).astype(f)
    t["sin"] = np.tile(np.sin(ang), (4, 1)).astype(f)
    i, k = np.arange(P)[:, None], np.arange(256)[None, :]
    t["mask_p"] = np.where((k >= i) & (k <= i + P), 0.0, -1e30).astype(f)
    s = np.arange(P)[:, None] % NS_S
    t["mask_c"] = np.where(np.arange(P)[None, :] >= s, 0.0, -1e30).astype(f)
    j = np.arange(64)[None, None, :]
    b = np.arange(NB_S)[None, :, None]
    t["mask_n"] = np.where((j // NS_S == b) & (j % NS_S <= s[:, :, None]), 0.0, -1e30).astype(f)
    lg = np.log1p(-np.exp2(-5.0 - np.arange(HR, dtype=f))).astype(f)
    jj, ii = np.arange(P)[:, None, None], np.arange(P)[None, None, :]
    t["intra"] = np.where(ii >= jj, np.exp(np.maximum(ii - jj, 0).astype(f) * lg[None, :, None]), 0).astype(f)
    jj, ii = np.arange(64)[:, None, None], np.arange(64)[None, None, :]
    same = (jj // 8 == ii // 8) & (ii >= jj)
    t["intra_s"] = np.zeros((P, HR, 64), f)
    t["intra_s"][:64] = np.where(same, np.exp(np.maximum(ii - jj, 0).astype(f) * lg[None, :, None]), 0)
    head = 2 * np.arange(4)[None, :] + np.arange(P)[:, None] // 64
    step = np.concatenate([np.arange(P), np.tile(np.arange(NS_S), NB_S)]).astype(f) + f(1)
    t["cross"] = np.exp(step[None, None, :] * lg[head][:, :, None]).astype(f)
    t["kdec"] = np.exp((P - 1 - np.arange(P, dtype=f))[:, None] * lg[None, :]).astype(f)
    t["mkd"] = np.zeros((P, HR, NB_S), f)
    r = np.arange(64)
    t["mkd"][:64] = np.where((r // 8)[:, None, None] == np.arange(NB_S)[None, None, :],
                             np.exp((NS_S - 1 - r % 8).astype(f)[:, None] * lg[None, :])[:, :, None], 0)
    t["cdec"] = np.stack([np.exp(f(P) * lg[head]), np.exp(f(NS_S) * lg[head])], 1).astype(f)
    return t


def _lay(w, kt, mt):
    K, M = w.shape
    a = w.reshape(K // (P * kt), kt, P, M // (P * mt), mt, P)
    return a.transpose(3, 0, 2, 4, 1, 5).reshape(-1, P, mt * kt * P)


def kernel(**inputs):
    import concourse.bacc as _bacc
    from concourse.bass_utils import run_bass_kernel_spmd as _run

    g = {n: np.asarray(a) for n, a in inputs.items()}
    f = np.float32
    heads = [(2 * (t // 4) + u) * 4 + t % 4 for t in range(8) for u in range(2)]
    w_in = g["w_in"][0]
    qa = w_in[:, :HA * DA].reshape(D, HA, DA)[:, heads].reshape(D, HA * DA)
    w_a = g["w_branch_attn"][0].reshape(HA, DA, D)[heads].reshape(HA * DA, D)
    br = np.stack([_lay(w_a, 8, 1), _lay(g["w_branch_ret"][0], 8, 1)], 1).reshape(-1, P, 8 * P)
    u_t = g["peer_u"][0].T
    ub = _lay(u_t, 8, 1).reshape(NG, 8, P, 8 * P)
    vb = np.stack([_lay(g["peer_v"][0][n * 512:(n + 1) * 512], 4, 2) for n in range(NG)])
    uv = [ub[0]]
    for n in range(NG - 1):
        uv += [ub[n + 1], vb[n]]
    uv.append(vb[NG - 1])
    w = np.concatenate([_lay(qa, 8, 1), _lay(w_in[:, HA * DA:], 8, 1), br, _lay(g["w_out"][0], 8, 1),
                        _lay(g["w_peer_query"][0], 8, 1), *uv, _lay(g["w_ple_proj"][0], 2, 4),
                        _lay(g["w_ple_gate"][0], 8, 1)])

    def feature_major(a, b, k):
        both = np.concatenate([a.reshape(-1, k * P), b.reshape(-1, k * P)])
        return both.T.reshape(k, P, T).transpose(1, 0, 2)

    sinks = g["attn_sinks"][0]
    arrays = dict(
        w=w, xT=feature_major(g["x_prompt"], g["x_sample"], KD), pT=feature_major(g["p_prompt"], g["p_sample"], 2),
        lns=np.stack([a.reshape(KD, P).T for a in (g["ln1"][0], g["ln2"][0], g["ln_ple"][0], g["ln_final"])], 1),
        ln_ret=g["ln_ret"][0].reshape(HR, P).T,
        sink_q=np.tile(sinks[heads].reshape(1, 8, 2), (P, 1, 1)), sink_r=np.repeat(sinks, 8)[:, None],
        sub_k=g["peer_sub_keys"][0].transpose(2, 0, 1),
        ckT=g["cache_k_win"][0].reshape(NB_S, P, 2, 2, DA).transpose(3, 4, 0, 2, 1).reshape(P, NB_S, 2, P),
        cache_k=g["cache_k_win"][0].reshape(NB_S, P, 256), cache_v=g["cache_v_win"][0].reshape(NB_S, P, 256),
        state=g["state_ret"][0].reshape(NB_S, 4, 2, DKR, DVR).transpose(2, 3, 1, 0, 4).reshape(P, 4, NB_S, DVR),
        **_tables())
    outs = dict(y=(P, KD, T), kc=(NB_S, P - NS_S, 256), vc=(NB_S, P - NS_S, 256), k_new=(P, 2, 192),
                v_new=(P, 2, 192), s_pr=(P, 4, DVR), s_smp=(P, 4, NB_S, DVR))
    nc = _bacc.Bacc("TRN2", target_bir_lowering=False, num_devices=1)
    d, o = {}, {}
    arrays = {n: np.ascontiguousarray(a) for n, a in arrays.items()}
    for n, a in arrays.items():
        d[n] = nc.dram_tensor("in_" + n, a.shape, mybir.dt.from_np(a.dtype), kind="ExternalInput").ap()
    for n, s in outs.items():
        o[n] = nc.dram_tensor("out_" + n, s, F32, kind="ExternalOutput").ap()
    d["spill"] = nc.dram_tensor("spill_scr", (N_SPILL, P, T), F32, kind="Internal").ap()
    d["g_scr"] = nc.dram_tensor("gate_scr", (NGT, P, NK, GT), F32, kind="Internal").ap()
    build(nc, d, o)
    r = _run(nc, [{"in_" + n: a for n, a in arrays.items()}], core_ids=[0]).results[0]
    r = {n: np.asarray(r["out_" + n]) for n in outs}

    y = r["y"].transpose(2, 1, 0).reshape(T, D)

    def window(a):
        return a.reshape(2, DA, 2, -1).transpose(3, 2, 0, 1).reshape(-1, KVA, DA)

    kn, vn = window(r["k_new"]), window(r["v_new"])
    k_p, v_p = kn[None, None, :P], vn[None, None, :P]
    k_s, v_s = (np.concatenate([c.reshape(NB_S, P - NS_S, KVA, DA), n[P:].reshape(NB_S, NS_S, KVA, DA)], 1)[None]
                for c, n in ((r["kc"], kn), (r["vc"], vn)))
    s_p = r["s_pr"].reshape(2, DKR, 4, DVR).transpose(2, 0, 1, 3).reshape(1, 1, HR, DKR, DVR)
    s_s = r["s_smp"].reshape(2, DKR, 4, NB_S, DVR).transpose(3, 2, 0, 1, 4).reshape(1, NB_S, HR, DKR, DVR)
    return (y[:NP_TOK].reshape(1, NP_TOK, D), y[NP_TOK:].reshape(NB_S, NS_S, D), k_p, v_p, s_p, k_s, v_s, s_s)
```

```python
from contextlib import ExitStack, contextmanager

import numpy as np
import concourse.bass as bass
from concourse import mybir

F32 = mybir.dt.float32
F32R = mybir.dt.float32r
U32 = mybir.dt.uint32
ALU = mybir.AluOpType
ACT = mybir.ActivationFunctionType
AX = mybir.AxisListType

P = 128
D = 2048
KD = D // P
NP_TOK, NB_S, NS_S = 512, 8, 8
T = NP_TOK + NB_S * NS_S
TH = T // 2
TT = 5
ROWS = [P] * 4 + [T - 4 * P]
HA, KVA, DA = 16, 4, 64
HR, DKR, DVR = 8, 64, 128
PH, NK, TOPK = 8, 128, 16
PAST = 2048
EPS = 1e-6

QA, KA, VA, QR, KR, VR = 0, 8, 10, 12, 16, 20
N_FEAT = 28
GR, GA, GB = 0, 8, 24
N_SPILL = 40

B_IN = 0
B_BR = B_IN + (N_FEAT + N_SPILL) * 2
B_O = B_BR + KD * 2
B_Q = B_O + KD * 2
B_U = B_Q + KD * 2
NCHUNK = NK
GRP = 4
NG = NCHUNK // GRP
GT = 48
NGT = T // GT
NPRE = 8
PRE = NPRE * GRP
PRE_A, PRE_B = PRE - NGT - 4, PRE - 4
B_V = B_U + PRE * 2
B_UV = B_V + (NPRE - 1) * 8
B_PG = B_U + 2 * NCHUNK * 2
N_BLOCKS = B_PG + 36

A_IN, A_BR = 0, N_FEAT
A_O = A_BR + 2 * KD
A_Q = A_O + KD
A_V = A_Q + KD
A_PG = A_V + NG * KD
R_IN, R_U = 0, N_SPILL
R_PG = R_U + NCHUNK

SCALE = DA ** -0.5


class Chain:

    def __init__(self, eng, sem):
        self.eng, self.sem, self.n, self.loops = eng, sem, 0, []

    def did(self, ins):
        ins.then_inc(self.sem, 1)
        self.n += 1

    def wait(self, back=0):
        v = self.n - back
        for reg, per in self.loops:
            v = reg * per + v
        self.eng.wait_ge(self.sem, v)

    @contextmanager
    def loop(self, count, per):
        with self.eng.Fori(0, count) as i:
            start = self.n
            self.loops.append((i, per))
            yield i
            self.loops.pop()
            assert self.n - start == per, (self.n - start, per)
        self.n = start + per * count


def at_step(base, loops, scale=1):
    v = base
    for reg, per in loops:
        v = reg * (per * scale) + v
    return v


def halves(ap):
    return ap.rearrange("p (a b) -> p a b", a=2)


def build(nc, d, o):
    ctx = ExitStack()
    with ctx:
        base = (nc.sbuf_base + 63) // 64 * 64
        limit = base + nc.sbuf_bytes_remaining - 64

        def at(name, shape, dt, offset):
            size = 4
            for s in shape[1:]:
                size *= s
            assert offset % 4 == 0 and base + offset + size <= limit, (name, offset, size, limit - base)
            return nc.alloc_sbuf_tensor_at(name, shape, dt, offset=base + offset)

        def run(start, *items):
            out = []
            for name, shape, dt in items:
                out.append(at(name, shape, dt, start))
                size = 4
                for s in shape[1:]:
                    size *= s
                start += (size + 31) // 32 * 32
            return out, start

        TB = T * 4
        (raw, whi, wlo), e = run(0, ("w_raw", [P, 2, 8, P], F32), ("w_hi", [P, 2, 8, P], F32R),
                                 ("w_lo", [P, 2, 8, P], F32R))
        (ones, ident, swap, iota, lns, ln_ret, sink_q, nsink_q, sink_r, nsink_r, sub_k, cdec, rms_m, rstd), e = run(
            e, ("ones", [P, P], F32), ("ident", [P, P], F32), ("swap", [P, P], F32), ("iota", [P, P], F32),
            ("lns", [P, 4, KD], F32), ("ln_ret_c", [P, HR], F32), ("sink_q", [P, 8, 2], F32),
            ("nsink_q", [P, 8, 2], F32), ("sink_r", [P, 1], F32), ("nsink_r", [P, 1], F32),
            ("sub_k", [P, 2, NK], F32), ("cdec", [P, 2, 4], F32), ("rms_m", [P, T], F32), ("rstd", [P, T], F32))
        gsp = at("gsp", [P, 2, T], F32, e - 2 * TB)
        rA = e
        rX = rA
        rM = rA + KD * TB
        rH = rA + 38 * TB
        rZ = rH + 32 * TB

        x = at("x", [P, KD, T], F32, rX)
        h_hi = at("h_hi", [P, KD, T], F32R, rH)
        h_lo = at("h_lo", [P, KD, T], F32R, rH + KD * TB)
        (sq, hf), _ = run(rZ, ("sq", [P, 2, T], F32), ("hf", [P, 4, T], F32))
        feat = at("feat", [P, N_FEAT, T], F32, rA)
        (cos_t, sin_t, spill), e = run(rA + N_FEAT * TB, ("cos_t", [P, T], F32), ("sin_t", [P, T], F32),
                                       ("spill", [P, 2, T], F32))
        (pT, att, s_prompt, qx, qs), rot_at = run(
            rA + (N_FEAT + 2) * TB, ("pT", [P, 2, 4, P], F32), ("att", [P, 2, 2, P], F32),
            ("s_prompt", [P, 4, P], F32), ("qx", [P, 2, P], F32), ("qs", [P, NB_S, 2, 4 * NS_S], F32))
        (rot_c, rot_s), _ = run(rot_at, ("rot_c", [P, T], F32), ("rot_s", [P, T], F32))
        (v_tok, k_tok, vr_tok, o_a, o_r), e = run(
            rH, ("v_tok", [P, TT, 256], F32), ("k_tok", [P, TT, HR, DKR], F32), ("vr_tok", [P, TT, HR, DVR], F32),
            ("o_a", [P, 8, T], F32), ("o_r", [P, HR, T], F32))
        (ck, cv), _ = run(e - HR * TB, ("ck", [P, NB_S, 2, P], F32),
                          ("cv", [P, NB_S, 256], F32))
        (mask_p, mask_c, mask_n, cross, kdec, mkd, sm, mx, sums, esink, den), _ = run(
            rZ, ("mask_p", [P, 256], F32),
            ("mask_c", [P, P], F32), ("mask_n", [P, NB_S, 64], F32), ("cross", [P, 4, 192], F32),
            ("kdec", [P, HR], F32), ("mkd", [P, HR, NB_S], F32), ("sm", [P, 2, 2, 256], F32),
            ("mx", [P, 2, 4], F32), ("sums", [P, 2, 2], F32), ("esink", [P, 2, 2], F32), ("den", [P, 2, 4], F32))
        s0 = [at(f"s0_{t}", [P, NB_S, P], F32, offset) for t, offset in enumerate(
            (rA + VR * TB, rA + VR * TB + NB_S * P * 4, rA + N_FEAT * TB, rot_at))]
        (intra, intra_s, kb), _ = run(
            rA + VR * TB + 2 * NB_S * P * 4, ("intra", [P, HR, P], F32),
            ("intra_s", [P, HR, 64], F32), ("kb", [P, 2, NB_S, DKR], F32))
        gn_d = at("gn_d", [P, 4, T], F32, rH)
        (gn_sq, gn_g, gn_ms, gn_rs), _ = run(
            rZ, ("gn_sq", [P, T], F32), ("gn_g", [P, 2, T], F32), ("gn_ms", [P, T], F32),
            ("gn_rs", [P, T], F32))
        gn_var, gn_root = (rms_m, gn_ms), (rstd, gn_rs)
        (oa_hi, oa_lo, or_hi, or_lo), e = run(rA, ("oa_hi", [P, 8, T], F32R), ("oa_lo", [P, 8, T], F32R),
                                              ("or_hi", [P, 8, T], F32R), ("or_lo", [P, 8, T], F32R))
        (g_ab,), _ = run(e, ("g_ab", [P, 2, 2, T], F32))
        (br_t,), _ = run(rZ, ("br_t", [P, 3, T], F32))
        (qf, work, tv, ti, wv, wi, comb, hot, bv, bi, bab, bf, gij, gmx), _ = run(
            rM, ("qf", [P, 2, T], F32), ("work", [P, TT, NK], F32), ("tv", [P, TT, 16, TOPK], F32),
            ("ti", [P, TT, 16, TOPK], F32), ("wv", [P, TT, TOPK], F32), ("wi", [P, TT, TOPK], U32),
            ("comb", [P, PH, 256], F32), ("hot", [P, P, TOPK], F32), ("bv", [P, TT, PH, TOPK], F32), ("bi", [P, P], U32),
            ("bab", [P, 2, P], U32), ("bf", [P, 2, P], F32), ("gij", [P, TT, 3, P], F32),
            ("gmx", [P, TT, PH], F32))
        (gij_t, oh_cur, oh_j, oh_i), _ = run(
            rZ, ("gij_t", [P, T, 3], F32), ("oh_cur", [P, 2, GT, 3], F32), ("oh_j", [P, 2, 4, P], F32),
            ("oh_i", [P, 2, 4, P], F32))
        g_st = at("g_st", [P, 2, NK, GT], F32, rM)
        (a_hi, a_lo, g_in, gl), _ = run(rM, ("a_hi", [P, 2, GRP, T], F32R), ("a_lo", [P, 2, GRP, T], F32R),
                                        ("g_in", [P, 2, NGT, 2, GT], F32), ("gl", [P, 2, T], F32))
        (af,), _ = run(rZ, ("af", [P, 2, T], F32))
        (p_hi, p_lo, proj, sg), _ = run(rM, ("p_hi", [P, 2, T], F32R), ("p_lo", [P, 2, T], F32R),
                                        ("proj", [P, KD, T], F32), ("sg", [P, 2, T], F32))
        p_raw = at("p_raw", [P, 2, T], F32, rZ + 4 * TB)
        PS = ctx.enter_context(nc.psum_tensor("PS", [P, 8, 512], F32))

        def ring_a(t):
            return PS[:, 2 * (t % 2):2 * (t % 2) + 2, 0:TH]

        def ring_b(t):
            return PS[:, 4 + 2 * (t % 2):6 + 2 * (t % 2), 0:TH]

        names = """raw0 raw1 hi lo used free_a free_b vt const tab ones x0 x1 x2 x3 x_again kv0 kv1 s0 s0_out gn0 gn1 gab0 gab1 gin0 gin1
            p p_done spill0 spill1 gput0 gput1 out win_out kv_out sp_out chain passed passed_pe passed_act
            sq sqm ms rt hf hhi h_done rot rotf rope tr_a tr_k tr_v trf_a trf_k trf_v
            as_mm as_m as_e as_p as_t as_tc as_o as_of bs_mm bs_m bs_e bs_p bs_t bs_tc bs_o bs_of
            rt_mm rt_at rt_qx rt_o rt_of rt_s rt_sf ro_c st_mm st_at st_kb st_o st_of st_s st_sf
            gn_mu gn_dd gn_q gn_v gn_vv gn_rt gn_done
            oah oab m_done sc_mm sc_f ft_x ft_e ft_g tr_g trf_g oh g_mm g_ev gl a_rdy pas asp0 asp1 gl0 gl1""".split()
        S = {n: ctx.enter_context(nc.semaphore("s_" + n)) for n in names}
        s_raw = [S["raw0"], S["raw1"]]
        s_hi, s_lo, s_used, s_free_a, s_free_b = S["hi"], S["lo"], S["used"], S["free_a"], S["free_b"]
        block = ctx.enter_context(nc.Block())

        @block.sync
        def _(sp):
            def loads(b0, b1):
                with sp.Fori(0, (b1 - b0) // 2) as i:
                    for u in range(2):
                        sp.wait_ge(s_lo, i * 2 + (b0 + u - 1))
                        sp.dma_start(raw[:, u].rearrange("p m c -> p (m c)"), d["w"][i * 2 + (b0 + u)]
                                     ).then_inc(s_raw[u], 16)

            for u in range(2):
                sp.dma_start(raw[:, u].rearrange("p m c -> p (m c)"), d["w"][u]).then_inc(s_raw[u], 16)
            loads(2, N_BLOCKS)
            for n in range(KD // 2):
                sp.wait_ge(S["h_done"], 3 * KD + 2 * n + 2)
                sp.dma_start(o["y"][:, 2 * n:2 * n + 2], x[:, 2 * n:2 * n + 2]).then_inc(S["out"], 16)
            sp.wait_ge(S["out"], 16 * (KD // 2))
            sp.wait_ge(S["win_out"], 32)
            sp.wait_ge(S["kv_out"], 32)
            sp.wait_ge(S["sp_out"], 16)
            for u in range(2):
                sp.wait_ge(S[f"spill{u}"], 16 * (N_SPILL // 2))
                sp.wait_ge(S[f"gput{u}"], 16 * (NGT // 2))
                sp.wait_ge(S["s0_out"], 64)
                sp.wait_ge(S[f"asp{u}"], 16 * (PRE // 2))

        @block.gpsimd
        def _(pool):
            const, tab, out = S["const"], S["tab"], S["win_out"]
            pool.dma_start(ones[:], d["ones"]).then_inc(S["ones"], 16)
            for q in range(4):
                pool.dma_start(x[:, 4 * q:4 * q + 4], d["xT"][:, 4 * q:4 * q + 4]).then_inc(S[f"x{q}"], 16)
            for dst, name in ((lns, "lns"), (ident, "ident"), (swap, "swap"), (iota, "iota"), (ln_ret, "ln_ret"), (sink_q, "sink_q"), (sink_r, "sink_r"), (sub_k, "sub_k"),
                              (cdec, "cdec")):
                pool.dma_start(dst[:], d[name]).then_inc(const, 16)
            pool.dma_start(o["kc"], d["cache_k"][:, NS_S:]).then_inc(out, 16)
            pool.dma_start(o["vc"], d["cache_v"][:, NS_S:]).then_inc(out, 16)
            with pool.Fori(0, N_SPILL // 2) as i:
                for u in range(2):
                    pool.wait_ge(s_free_b, i * 2 + (u + 1))
                    pool.dma_start(d["spill"][i * 2 + u], spill[:, u]).then_inc(S[f"spill{u}"], 16)
            pool.wait_ge(s_used, B_BR)
            for dst, name in ((cos_t, "cos"), (sin_t, "sin"), (mask_p, "mask_p"), (mask_c, "mask_c"),
                              (mask_n, "mask_n"), (cross, "cross"), (kdec, "kdec"), (mkd, "mkd")):
                pool.dma_start(dst[:], d[name]).then_inc(tab, 16)
            pool.dma_start(ck[:], d["ckT"]).then_inc(S["kv0"], 16)
            pool.dma_start(cv[:], d["cache_v"].rearrange("b p c -> p b c")).then_inc(S["kv1"], 16)
            pool.wait_ge(S["rope"], 10)
            pool.dma_start(o["k_new"], feat[:, KA:KA + 2, 384:T]).then_inc(S["kv_out"], 16)
            pool.dma_start(o["v_new"], feat[:, VA:VA + 2, 384:T]).then_inc(S["kv_out"], 16)
            pool.wait_ge(S["tr_v"], TT)
            pool.dma_start(intra[:], d["intra"]).then_inc(tab, 16)
            pool.dma_start(intra_s[:], d["intra_s"]).then_inc(tab, 16)
            pool.wait_ge(S["rope"], 18)
            for t in range(4):
                pool.dma_start(s0[t][:], d["state"][:, t]).then_inc(S["s0"], 16)
            pool.wait_ge(S["rt_sf"], 16)
            pool.dma_start(o["s_pr"], s_prompt[:]).then_inc(S["sp_out"], 16)
            for t in range(4):
                pool.wait_ge(S["st_sf"], 2 * t + 2)
                pool.dma_start(o["s_smp"][:, t], s0[t][:]).then_inc(S["s0_out"], 16)
            for u in range(2):
                pool.wait_ge(S[f"spill{u}"], 16 * (N_SPILL // 2))
            pool.wait_ge(S["gn_dd"], 1)
            for h in range(HR):
                if h >= 2:
                    pool.wait_ge(S["gn_done"], h - 1)
                pool.dma_start(gn_g[:, h % 2], d["spill"][GR + h]).then_inc(S[f"gn{h % 2}"], 16)
                pool.wait_ge(S["oah"], h + 1)
                nc.gpsimd.tensor_tensor(oa_lo[:, h], o_a[:, h], oa_hi[:, h].bitcast(F32), ALU.subtract
                                        ).then_inc(S["oab"], 1)
            pool.wait_ge(S["oab"], 8)
            pool.wait_ge(S["sp_out"], 16)
            for u in range(2):
                for r in range(2):
                    pool.dma_start(g_ab[:, u, r], d["spill"][u + (GA if r == 0 else GB)]).then_inc(S[f"gab{u}"], 16)
            with pool.Fori(1, KD // 2) as i:
                for u in range(2):
                    pool.wait_ge(S["m_done"], i * 2 + (u - 1))
                    for r in range(2):
                        pool.dma_start(g_ab[:, u, r], d["spill"][i * 2 + (u + (GA if r == 0 else GB))]
                                       ).then_inc(S[f"gab{u}"], 16)
            pool.wait_ge(s_used, B_O)
            pool.dma_start(x[:], d["xT"]).then_inc(S["x_again"], 16)

            def split(b, loops=()):
                pool.wait_ge(s_hi, at_step(b + 1, loops))
                nc.gpsimd.tensor_tensor(wlo[:, b % 2], raw[:, b % 2], whi[:, b % 2].bitcast(F32), ALU.subtract
                                        ).then_inc(s_lo, 1)

            def put(t, loops=()):
                bl, tl = [(r, 4) for r in loops], [(r, 2) for r in loops]
                split(B_U + 2 * t + 2, bl)
                split(B_U + 2 * t + 3, bl)
                pool.wait_ge(s_free_b, at_step(N_SPILL + t + 1, tl))
                pool.dma_start(d["asp"][at_step(t, tl)], gsp[:, t % 2]).then_inc(S[f"asp{t % 2}"], 16)

            pool.wait_ge(s_lo, B_U + 2)
            with pool.Fori(0, PRE_A // 2) as i:
                for u in range(2):
                    put(u, [i])
            with pool.Fori(0, NGT // 2) as i:
                for u in range(2):
                    put(PRE_A + u, [i])
                    pool.wait_ge(S["g_ev"], i * 24 + (12 * u + 14))
                    pool.dma_start(d["g_scr"][i * 2 + u], g_st[:, u]).then_inc(S[f"gput{u}"], 16)
            def gates(q, u):
                pool.dma_start(g_in[:, u], d["g_scr"][:, :, bass.ds(q * 2, 2)].rearrange("b j i t -> j b i t")
                               ).then_inc(S[f"gin{u}"], 16)

            def acts(t, u):
                pool.wait_ge(S["gl"], t + 1)
                pool.dma_start(gl[:, u], d["asp"][t]).then_inc(S[f"gl{u}"], 16)

            put(PRE_B)
            put(PRE_B + 1)
            for u in range(2):
                pool.wait_ge(S[f"gput{u}"], 16 * (NGT // 2))
                pool.wait_ge(S[f"asp{u}"], 16 * (PRE_B // 2))
            for u in range(2):
                acts(u, u)
                gates(u, u)
            acts(2, 0)
            acts(3, 1)
            gates(2, 0)
            put(PRE_B + 2)
            put(PRE_B + 3)
            for u in range(2):
                pool.wait_ge(S[f"asp{u}"], 16 * (PRE // 2))
            acts(4, 0)
            acts(5, 1)
            gates(3, 1)
            with pool.Fori(2, PRE // 4) as i:
                for u in range(2):
                    acts(i * 4 + (2 * u - 2), 0)
                    acts(i * 4 + (2 * u - 1), 1)
                    gates(i * 2 + u, u)
            acts(PRE - 2, 0)
            acts(PRE - 1, 1)
            gates(PRE // 2, 0)
            pool.wait_ge(S["gl"], PRE + 2)
            gates(PRE // 2 + 1, 1)
            with pool.Fori(PRE // 4 + 1, NCHUNK // 4) as i:
                for u in range(2):
                    pool.wait_ge(S["gl"], i * 4 + 2 * u)
                    gates(i * 2 + u, u)
            pool.wait_ge(s_used, B_PG)
            pool.dma_start(p_raw[:], d["pT"]).then_inc(S["p"], 16)

        @block.scalar
        def _(act):
            def split(b, loops=()):
                act.wait_ge(s_raw[b % 2], at_step(16 * (b // 2 + 1), loops, 8))
                if b >= 2:
                    act.wait_ge(s_used, at_step(b - 1, loops))
                nc.scalar.activation(whi[:, b % 2], raw[:, b % 2], ACT.Copy).then_inc(s_hi, 1)

            def norm(r):
                with act.Fori(0, KD // 2) as i:
                    for u in range(2):
                        act.wait_ge(S["sqm"], i * 2 + (KD * r + u + 1))
                        nc.scalar.activation(sq[:, u], x[:, i * 2 + u], ACT.Square).then_inc(S["sq"], 1)
                roots(r)

            def roots(r):
                act.wait_ge(S["ms"], r + 1)
                nc.scalar.activation(rstd[:], rms_m[:], ACT.Sqrt).then_inc(S["rt"], 1)
                if r < 3:
                    with act.Fori(0, KD // 4) as i:
                        for u in range(4):
                            act.wait_ge(S["hf"], i * 4 + (KD * r + u + 1))
                            nc.scalar.activation(h_hi[:, i * 4 + u], hf[:, u], ACT.Copy).then_inc(S["hhi"], 1)

            split(0)
            split(1)
            for k in range(KD):
                if k % 4 == 0:
                    act.wait_ge(S[f"x{k // 4}"], 16)
                act.wait_ge(S["sqm"], k + 1)
                nc.scalar.activation(sq[:, k % 2], x[:, k], ACT.Square).then_inc(S["sq"], 1)
            roots(0)
            with act.Fori(0, N_FEAT) as i:
                split(2, [(i, 2)])
                split(3, [(i, 2)])

            def spilled(n, t0, func):
                def one(t, loops=()):
                    b = 2 * (N_FEAT + t)
                    split(b + 2, [(r, 4) for r in loops])
                    split(b + 3, [(r, 4) for r in loops])
                    if t >= 2:
                        act.wait_ge(S[f"spill{t % 2}"], at_step(16 * (t // 2), [(r, 1) for r in loops], 16))
                    nc.scalar.activation(halves(spill[:, t % 2]), ring_b(t), func).then_inc(s_free_b, 1)

                one(t0)
                one(t0 + 1)
                with act.Fori(0, n // 2 - 1) as i:
                    one(t0 + 2, [i])
                    one(t0 + 3, [i])

            spilled(8, 0, ACT.Silu)
            spilled(32, 8, ACT.Sigmoid)

            act.wait_ge(S["const"], 144)
            nc.scalar.activation(nsink_q[:], sink_q[:], ACT.Copy, scale=-1.0).then_inc(S["as_e"], 1)
            nc.scalar.activation(nsink_r[:], sink_r[:], ACT.Copy, scale=-1.0).then_inc(S["as_e"], 1)
            for tt in range(TT):
                n = ROWS[tt]
                act.wait_ge(S["tr_v"], tt + 1)
                nc.scalar.activation(vr_tok[0:n, tt].rearrange("p (a h) v -> p a (h v)", a=2), PS[0:n, 6:8, :],
                                     ACT.Copy).then_inc(S["trf_v"], 1)

            def exps(n):
                act.wait_ge(S["as_m"], n + 1)
                w = 128 if n % 4 == 0 else 256
                for u in range(2):
                    nc.scalar.activation(sm[:, n % 2, u, 0:w], sm[:, n % 2, u, 0:w], ACT.Exp,
                                         bias=mx[:, n % 2, 2 + u:3 + u],
                                         accum_out=sums[:, n % 2, u:u + 1]).then_inc(S["as_e"], 1)
                    nc.scalar.activation(esink[:, n % 2, u:u + 1], sink_q[:, n // 4, u:u + 1], ACT.Exp,
                                         bias=mx[:, n % 2, 2 + u:3 + u]).then_inc(S["as_e"], 1)

            def copy_pt(n):
                act.wait_ge(S["as_t"], n + 1)
                if n >= 2:
                    act.wait_ge(S["as_o"], n - 1)
                k = 2 if n % 4 == 0 else 4
                nc.scalar.activation(pT[:, n % 2, 0:k], PS[:, 4 + n % 2, 0:128 * k].rearrange(
                    "p (a b) -> p a b", b=P), ACT.Copy).then_inc(S["as_tc"], 1)

            for u in range(2):
                act.wait_ge(S[f"spill{u}"], 16 * (N_SPILL // 2))
            for n in range(32 + 1):
                if n < 32:
                    exps(n)
                if n >= 1:
                    copy_pt(n - 1)

            def exps_s(b):
                act.wait_ge(S["bs_m"], b + 1)
                nc.scalar.activation(sm[:, b % 2, 0, 0:192], sm[:, b % 2, 0, 0:192], ACT.Exp,
                                     bias=mx[:, b % 2, 1:2], accum_out=sums[:, b % 2, 0:1]).then_inc(S["bs_e"], 1)
                nc.scalar.activation(esink[:, b % 2, 0:1], sink_r[:], ACT.Exp,
                                     bias=mx[:, b % 2, 1:2]).then_inc(S["bs_e"], 1)

            def copy_pts(b):
                act.wait_ge(S["bs_t"], b + 1)
                if b >= 2:
                    act.wait_ge(S["bs_o"], b - 1)
                else:
                    act.wait_ge(S["as_o"], 32)
                nc.scalar.activation(pT[:, b % 2, 0], PS[:, 4 + b % 2, 0:P], ACT.Copy).then_inc(S["bs_tc"], 1)
                nc.scalar.activation(pT[0:64, b % 2, 1], PS[0:64, 4 + b % 2, P:2 * P], ACT.Copy
                                     ).then_inc(S["bs_tc"], 1)

            for b in range(NB_S + 1):
                if b < NB_S:
                    exps_s(b)
                if b >= 1:
                    copy_pts(b - 1)

            for n in range(16):
                c, t = n // 4, n % 4
                act.wait_ge(S["rt_o"], n + 1)
                nc.scalar.activation(o_r[:, 2 * t:2 * t + 2, c * P:(c + 1) * P], PS[:, 2:4, 0:P],
                                     ACT.Copy).then_inc(S["ro_c"], 1)
            for t in range(4):
                act.wait_ge(S["st_o"], t + 1)
                nc.scalar.activation(o_r[:, 2 * t:2 * t + 2, NP_TOK:T], PS[:, 2:4, 0:64],
                                     ACT.Copy).then_inc(S["ro_c"], 1)

            for h in range(HR + 1):
                if h < HR:
                    act.wait_ge(S["gn_dd"], h + 1)
                    nc.scalar.activation(oa_hi[:, h], o_a[:, h], ACT.Copy).then_inc(S["oah"], 1)
                    if h >= 1:
                        act.wait_ge(S["gn_v"], h)
                    nc.scalar.activation(gn_sq[:], gn_d[:, h % 4], ACT.Square).then_inc(S["gn_q"], 1)
                if h >= 1:
                    act.wait_ge(S["gn_vv"], h)
                    nc.scalar.activation(gn_root[(h - 1) % 2][:], gn_var[(h - 1) % 2][:], ACT.Sqrt
                                         ).then_inc(S["gn_rt"], 1)

            def weights(b0, n, loops=()):
                with act.Fori(0, n) as j:
                    split(b0, [*loops, (j, 2)])
                    split(b0 + 1, [*loops, (j, 2)])

            weights(B_BR + 2, (B_Q - B_BR) // 2)
            act.wait_ge(s_free_a, A_Q)
            norm(1)
            weights(B_Q + 2, (B_U - B_Q) // 2)
            def gelu_out(t, loops=()):
                if t >= 2:
                    act.wait_ge(S[f"asp{t % 2}"], at_step(16 * (t // 2), loops, 16))
                nc.scalar.activation(halves(gsp[:, t % 2]), ring_b(t), ACT.Gelu).then_inc(s_free_b, 1)

            def plain(t, loops=()):
                bl = [(r, 4) for r in loops]
                split(B_U + 2 * t + 2, bl)
                split(B_U + 2 * t + 3, bl)
                gelu_out(t, [(r, 1) for r in loops])

            plain(0)
            plain(1)
            with act.Fori(0, PRE_A // 2 - 2) as i:
                for u in range(2):
                    plain(2 + u, [i])
            for tt in range(TT):
                act.wait_ge(S["ft_x"], tt + 1)
                nc.scalar.activation(bv[0:ROWS[tt], tt], bv[0:ROWS[tt], tt], ACT.Exp).then_inc(S["ft_e"], 1)
            plain(PRE_A - 2)
            plain(PRE_A - 1)

            act.sem_inc(S["g_ev"], 2)

            def beside(s, loops=()):
                t = PRE_A + s
                bl, ul = [(r, 4) for r in loops], [(r, 24) for r in loops]
                if s >= 2:
                    act.wait_ge(S[f"gput{s % 2}"], at_step(16, [(r, 1) for r in loops], 16))
                for half in range(2):
                    for n in range(6 * half, 6 * half + 6):
                        act.wait_ge(S["g_mm"], at_step(12 * s + n + 3, ul))
                        nc.scalar.activation(g_st[:, s % 2, :, 4 * n:4 * n + 4],
                                             PS[:, n % 2, :].rearrange("p (t i) -> p i t", t=4), ACT.Copy
                                             ).then_inc(S["g_ev"], 1)
                    split(B_U + 2 * t + 2 + half, bl)
                gelu_out(t, [(r, 1) for r in loops])

            beside(0)
            beside(1)
            with act.Fori(0, NGT // 2 - 1) as i:
                for s in range(2):
                    beside(2 + s, [i])
            with act.Fori(0, (PRE - PRE_B) // 2) as i:
                for u in range(2):
                    plain(PRE_B + u, [i])
            weights(B_V + 2, 4 * (NPRE - 1))

            def chunks(b0, t0, loops=()):
                with act.Fori(0, GRP // 2) as j:
                    for u in range(2):
                        bl = [*[(r, 16 * n) for r, n in loops], (j, 4)]
                        tl = [*[(r, GRP * n) for r, n in loops], (j, 2)]
                        split(b0 + 2 * u + 2, bl)
                        split(b0 + 2 * u + 3, bl)
                        act.wait_ge(S["gl"], at_step(t0 + u + 1, tl))
                        nc.scalar.activation(halves(gl[:, u]), ring_b(u), ACT.Gelu).then_inc(s_free_b, 1)

            with act.Fori(0, (NG - NPRE) // 2) as i:
                for g in range(2):
                    chunks(B_UV + 16 * g, GRP * (NPRE + g), [(i, 2)])
                    weights(B_UV + 10 + 16 * g, 4, [(i, 32)])
            weights(B_PG - 6, 4)

            weights(B_PG + 2, 2)
            act.wait_ge(s_free_a, A_PG)
            norm(2)
            with act.Fori(0, KD // 2 - 1) as i:
                for u in range(2):
                    split(B_PG + 6 + 2 * u, [(i, 4)])
                    split(B_PG + 7 + 2 * u, [(i, 4)])
                    act.wait_ge(S["pas"], i * 2 + (u + 1))
                    nc.scalar.activation(halves(sg[:, u]), ring_b(u), ACT.Sigmoid).then_inc(s_free_b, 1)
            for n in (KD - 2, KD - 1):
                if n == KD - 2:
                    split(N_BLOCKS - 2)
                    split(N_BLOCKS - 1)
                act.wait_ge(s_used, B_PG + 4 + 2 * n + 2)
                act.wait_ge(S["pas"], n + 1)
                nc.scalar.activation(halves(sg[:, n % 2]), ring_b(n), ACT.Sigmoid).then_inc(s_free_b, 1)
            act.wait_ge(S["pas"], KD + 2)
            norm(3)

        @block.vector
        def _(dve):
            ch = Chain(dve, S["chain"])
            v = nc.vector

            def split(b, loops=()):
                dve.wait_ge(s_hi, at_step(b + 1, loops))
                v.tensor_tensor(wlo[:, b % 2], raw[:, b % 2], whi[:, b % 2].bitcast(F32), ALU.subtract
                                ).then_inc(s_lo, 1)

            def hi_lo(src, hi, lo):
                ch.did(v.tensor_copy(hi, src))
                ch.wait()
                return v.tensor_tensor(lo, src, hi.bitcast(F32), ALU.subtract)

            def inverse_root(rstd=rstd, rms_m=rms_m):
                ch.did(v.reciprocal(rstd[:], rstd[:]))
                ch.wait()
                ch.did(v.scalar_tensor_tensor(rms_m[:], rms_m[:], -0.5, rstd[:], ALU.mult, ALU.mult))
                ch.wait()
                ch.did(v.tensor_tensor(rms_m[:], rms_m[:], rstd[:], ALU.mult))
                ch.wait()
                ch.did(v.scalar_tensor_tensor(rstd[:], rms_m[:], 1.5, rstd[:], ALU.add, ALU.mult))
                ch.wait()

            def norm(r, split_too):
                dve.wait_ge(S["sqm"], KD * (r + 1) + 2)
                v.tensor_scalar(halves(rms_m[:]), PS[:, 4:6, 0:TH], 1.0 / D, EPS, ALU.mult, ALU.add
                                ).then_inc(S["ms"], 1)
                dve.wait_ge(S["rt"], r + 1)
                inverse_root()
                if split_too:
                    def scaled(k, u):
                        v.scalar_tensor_tensor(hf[:, u], x[:, k], lns[:, r, bass.ds(k, 1)], rstd[:], ALU.mult, ALU.mult
                                               ).then_inc(S["hf"], 1)

                    def low(k, u):
                        dve.wait_ge(S["hhi"], k + (KD * r + 1))
                        v.tensor_tensor(h_lo[:, k], hf[:, u], h_hi[:, k].bitcast(F32), ALU.subtract
                                        ).then_inc(S["h_done"], 1)

                    scaled(0, 0)
                    scaled(1, 1)
                    low(0, 0)
                    scaled(2, 2)
                    low(1, 1)
                    scaled(3, 3)
                    with dve.Fori(0, KD // 4 - 1) as i:
                        for u in range(4):
                            low(i * 4 + (u + 2), (u + 2) % 4)
                            dve.wait_ge(S["h_done"], i * 4 + (KD * r + u + 1))
                            scaled(i * 4 + (u + 4), u)
                    low(KD - 2, 2)
                    low(KD - 1, 3)
                else:
                    with dve.Fori(0, KD // 2) as i:
                        for u in range(2):
                            v.scalar_tensor_tensor(x[:, i * 2 + u], x[:, i * 2 + u], lns[:, r, bass.ds(i * 2 + u, 1)],
                                                   rstd[:], ALU.mult, ALU.mult).then_inc(S["h_done"], 1)

            def weights(b0, n, loops=()):
                with dve.Fori(0, n) as j:
                    split(b0, [*loops, (j, 2)])
                    split(b0 + 1, [*loops, (j, 2)])

            split(0)
            split(1)
            dve.wait_ge(S["const"], 144)
            norm(0, True)
            with dve.Fori(0, N_FEAT // 2) as i:
                for u in range(2):
                    split(2 * u + 2, [(i, 4)])
                    split(2 * u + 3, [(i, 4)])
                    v.tensor_copy(halves(feat[:, i * 2 + u]), ring_a(u)).then_inc(s_free_a, 1)
            weights(2 * N_FEAT + 2, N_SPILL)
            dve.wait_ge(s_free_a, N_FEAT)

            dve.wait_ge(S["tab"], 16 * 8)
            ROPE = list(range(QA, KA + 2)) + list(range(QR, KR + 4))
            for r, f in enumerate(ROPE):
                s = DKR ** -0.5 if f >= KR else 1.0
                ch.did(v.scalar_tensor_tensor(rot_c[:], feat[:, f], s, cos_t[:], ALU.mult, ALU.mult))
                dve.wait_ge(S["rot"], r + 1)
                v.scalar_tensor_tensor(halves(rot_s[:]), PS[:, 2 * (r % 2):2 * (r % 2) + 2, 0:TH], s,
                                       halves(sin_t[:]), ALU.mult, ALU.mult).then_inc(S["rotf"], 1)
                ch.wait()
                dve.wait_ge(S["rotf"], r + 1)
                v.tensor_tensor(feat[:, f], rot_c[:], rot_s[:], ALU.add).then_inc(S["rope"], 1)
                dve.wait_ge(S["rope"], r + 1)
            for tt in range(TT):
                n = ROWS[tt]
                dve.wait_ge(S["tr_a"], tt + 1)
                v.tensor_copy(v_tok[0:n, tt], PS[0:n, 4, 0:256]).then_inc(S["trf_a"], 1)
                dve.wait_ge(S["tr_k"], tt + 1)
                src = PS[0:n, 5, :].rearrange("p (h k) -> p h k", h=HR)
                if tt < 4:
                    v.tensor_tensor(k_tok[0:n, tt], src, kdec[0:n, :].unsqueeze(2).broadcast_to([n, HR, DKR]),
                                    ALU.mult).then_inc(S["trf_k"], 1)
                else:
                    v.tensor_copy(k_tok[0:n, tt], src).then_inc(S["trf_k"], 1)

            def a_mask(n):
                w = 128 if n % 4 == 0 else 256
                q = n % 2
                dve.wait_ge(S["as_mm"], n + 1)
                if n >= 2:
                    dve.wait_ge(S["as_t"], n - 1)
                m = mask_p[:, 256 - w:256].unsqueeze(1).broadcast_to([P, 2, w])
                ch.did(v.scalar_tensor_tensor(sm[:, q, :, 0:w], PS[:, 2 * q:2 * q + 2, 0:w], SCALE, m,
                                              ALU.mult, ALU.add))
                ch.wait()
                ch.did(v.tensor_reduce(mx[:, q, 0:2], sm[:, q, :, 0:w], AX.X, ALU.max, negate=True))
                ch.wait()
                v.tensor_tensor(mx[:, q, 2:4], mx[:, q, 0:2], nsink_q[:, n // 4], ALU.min).then_inc(S["as_m"], 1)

            def a_prob(n):
                w = 128 if n % 4 == 0 else 256
                q = n % 2
                dve.wait_ge(S["as_e"], 4 * n + 6)
                ch.did(v.tensor_tensor(den[:, q, 0:2], sums[:, q], esink[:, q], ALU.add))
                ch.wait()
                ch.did(v.reciprocal(den[:, q, 2:4], den[:, q, 0:2]))
                ch.wait()
                v.tensor_tensor(sm[:, q, :, 0:w], sm[:, q, :, 0:w], den[:, q, 2:4].unsqueeze(2).broadcast_to([P, 2, w]),
                                ALU.mult).then_inc(S["as_p"], 1)

            def a_out(n):
                dve.wait_ge(S["as_o"], n + 1)
                v.tensor_copy(o_a[:, n // 4, (n % 4) * P:(n % 4 + 1) * P], PS[:, 6 + n % 2, 0:P]
                              ).then_inc(S["as_of"], 1)

            for p in range(2):
                ch.did(v.tensor_copy(qs[:, :, p].rearrange("p b (g s) -> p g b s", g=4),
                                     feat[:, QA + 4 * p:QA + 4 * p + 4, NP_TOK:T].rearrange(
                                         "p g (b s) -> p g b s", b=NB_S)))
            dve.wait_ge(S["as_e"], 2)
            for n in range(32 + 3):
                if n < 32:
                    a_mask(n)
                if 1 <= n < 33:
                    a_prob(n - 1)
                if n >= 3:
                    a_out(n - 3)

            def b_mask(b):
                q = b % 2
                dve.wait_ge(S["bs_mm"], b + 1)
                if b >= 2:
                    dve.wait_ge(S["bs_t"], b - 1)
                else:
                    dve.wait_ge(S["as_t"], 32)
                for kv in range(KVA):
                    r = slice(32 * kv, 32 * kv + 32)
                    bank = 2 * q + kv % 2
                    ch.did(v.scalar_tensor_tensor(sm[r, q, 0, 0:128], PS[r, bank, 0:128], SCALE, mask_c[r, :],
                                                  ALU.mult, ALU.add))
                    ch.did(v.scalar_tensor_tensor(sm[r, q, 0, 128:192], PS[r, bank, 128:192], SCALE,
                                                  mask_n[r, b], ALU.mult, ALU.add))
                ch.wait()
                ch.did(v.tensor_reduce(mx[:, q, 0:1], sm[:, q, 0, 0:192], AX.X, ALU.max, negate=True))
                ch.wait()
                v.tensor_tensor(mx[:, q, 1:2], mx[:, q, 0:1], nsink_r[:], ALU.min).then_inc(S["bs_m"], 1)

            def b_prob(b):
                q = b % 2
                dve.wait_ge(S["bs_e"], 2 * b + 2)
                ch.did(v.tensor_tensor(den[:, q, 0:1], sums[:, q, 0:1], esink[:, q, 0:1], ALU.add))
                ch.wait()
                ch.did(v.reciprocal(den[:, q, 1:2], den[:, q, 0:1]))
                ch.wait()
                v.tensor_scalar(sm[:, q, 0, 0:192], sm[:, q, 0, 0:192], den[:, q, 1:2], None, ALU.mult
                                ).then_inc(S["bs_p"], 1)

            def b_out(b):
                dve.wait_ge(S["bs_o"], b + 1)
                v.tensor_copy(o_a[:, :, NP_TOK + 8 * b:NP_TOK + 8 * b + 8],
                              PS[:, 6 + b % 2, 0:64].rearrange("p (g s) -> p g s", s=8)).then_inc(S["bs_of"], 1)

            for b in range(NB_S + 3):
                if b < NB_S:
                    b_mask(b)
                if 1 <= b < NB_S + 1:
                    b_prob(b - 1)
                if b >= 3:
                    b_out(b - 3)

            dve.wait_ge(S["tab"], 16 * 10)
            for n in range(16):
                c, t = n // 4, n % 4
                cols = slice(c * P, (c + 1) * P)
                if n >= 2:
                    dve.wait_ge(S["rt_o"], n - 1)
                v.tensor_tensor(qx[:, n % 2], feat[:, QR + t, cols], cross[:, t, 0:P], ALU.mult
                                ).then_inc(S["rt_qx"], 1)
                dve.wait_ge(S["rt_mm"], n + 1)
                v.tensor_tensor(att[:, n % 2], PS[:, 0:2, 0:P], intra[:, 2 * t:2 * t + 2], ALU.mult
                                ).then_inc(S["rt_at"], 1)
                dve.wait_ge(S["rt_s"], n + 1)
                if c == 0:
                    v.tensor_copy(s_prompt[:, t], PS[:, 6, 0:P]).then_inc(S["rt_sf"], 1)
                else:
                    dve.wait_ge(S["rt_sf"], n - 3)
                    v.scalar_tensor_tensor(s_prompt[:, t], s_prompt[:, t], cdec[:, 0, t:t + 1], PS[:, 6, 0:P],
                                           ALU.mult, ALU.add).then_inc(S["rt_sf"], 1)
                    dve.wait_ge(S["ro_c"], n + 1)
                    dst = o_r[:, 2 * t:2 * t + 2, cols]
                    v.tensor_tensor(dst, dst, PS[:, 4:6, 0:P], ALU.add).then_inc(S["rt_of"], 1)
            for t in range(4):
                if t < 2:
                    dve.wait_ge(S["rt_o"], 16)
                else:
                    dve.wait_ge(S["st_o"], t - 1)
                v.tensor_tensor(qx[:, t % 2, 0:64], feat[:, QR + t, NP_TOK:T], cross[:, t, P:P + 64], ALU.mult
                                ).then_inc(S["rt_qx"], 1)
                dve.wait_ge(S["st_mm"], t + 1)
                v.tensor_tensor(att[0:64, t % 2, :, 0:64], PS[0:64, 0:2, 0:64], intra_s[0:64, 2 * t:2 * t + 2],
                                ALU.mult).then_inc(S["st_at"], 1)
                if t:
                    dve.wait_ge(S["st_s"], 2 * t)
                for u in range(2):
                    h = 2 * t + u
                    v.tensor_tensor(kb[0:64, u], k_tok[0:64, 4, h].unsqueeze(1).broadcast_to([64, NB_S, DKR]),
                                    mkd[0:64, h].unsqueeze(2).broadcast_to([64, NB_S, DKR]), ALU.mult
                                    ).then_inc(S["st_kb"], 1)
                dve.wait_ge(S["ro_c"], 16 + t + 1)
                dst = o_r[:, 2 * t:2 * t + 2, NP_TOK:T]
                v.tensor_tensor(dst, dst, PS[:, 4:6, 0:64], ALU.add).then_inc(S["st_of"], 1)
                dve.wait_ge(S["s0"], 64)
                for q in range(2):
                    dve.wait_ge(S["st_s"], 2 * t + q + 1)
                    st = s0[t][:, 4 * q:4 * q + 4]
                    v.scalar_tensor_tensor(st, st, cdec[:, 1, t:t + 1],
                                           PS[:, 6 + q, :].rearrange("p (b v) -> p b v", b=4),
                                           ALU.mult, ALU.add).then_inc(S["st_sf"], 1)

            dve.wait_ge(S["st_sf"], 8)
            dve.wait_ge(S["st_of"], 4)
            dve.wait_ge(S["rt_of"], 12)
            dve.wait_ge(S["kv_out"], 32)
            dve.wait_ge(S["s0_out"], 64)
            def centred(h):
                dve.wait_ge(S["gn_mu"], h + 1)
                b = 4 * (h % 2)
                v.scalar_tensor_tensor(halves(gn_d[:, h % 4]), PS[:, b:b + 2, 0:TH], -1.0 / DVR, halves(o_r[:, h]),
                                       ALU.mult, ALU.add).then_inc(S["gn_dd"], 1)

            def variance(h):
                dve.wait_ge(S["gn_v"], h + 1)
                b = 4 * (h % 2) + 2
                v.tensor_scalar(halves(gn_var[h % 2][:]), PS[:, b:b + 2, 0:TH], 1.0 / DVR, EPS, ALU.mult, ALU.add
                                ).then_inc(S["gn_vv"], 1)

            for h in range(2):
                centred(h)
            for p in range(HR // 2):
                pair = (2 * p, 2 * p + 1)
                for h in pair:
                    variance(h)
                if p < HR // 2 - 1:
                    for h in pair:
                        centred(h + 2)
                dve.wait_ge(S["gn_rt"], 2 * p + 2)

                def step(make):
                    for u, h in enumerate(pair):
                        ch.wait(back=1)
                        ch.did(make(gn_d[:, h % 4], gn_root[u], gn_var[u], h))

                step(lambda dd, rs, ms, h: v.reciprocal(rs[:], rs[:]))
                step(lambda dd, rs, ms, h: v.scalar_tensor_tensor(ms[:], ms[:], -0.5, rs[:], ALU.mult, ALU.mult))
                step(lambda dd, rs, ms, h: v.tensor_tensor(ms[:], ms[:], rs[:], ALU.mult))
                step(lambda dd, rs, ms, h: v.scalar_tensor_tensor(rs[:], ms[:], 1.5, rs[:], ALU.add, ALU.mult))
                step(lambda dd, rs, ms, h: v.scalar_tensor_tensor(dd, dd, ln_ret[:, h:h + 1], rs[:],
                                                                  ALU.mult, ALU.mult))
                for u in range(2):
                    dve.wait_ge(S[f"gn{u}"], 16 * (p + 1))
                step(lambda dd, rs, ms, h: v.tensor_tensor(dd, dd, gn_g[:, h % 2], ALU.mult))
                step(lambda dd, rs, ms, h: v.tensor_copy(or_hi[:, h], dd))
                for h in pair:
                    ch.wait(back=1 - h % 2)
                    v.tensor_tensor(or_lo[:, h], gn_d[:, h % 4], or_hi[:, h].bitcast(F32), ALU.subtract
                                    ).then_inc(S["gn_done"], 1)
                dve.wait_ge(S["gn_done"], 2 * p + 2)

            with ch.loop(KD // 2, 4) as i:
                for u in range(2):
                    dve.wait_ge(S[f"gab{u}"], i * 32 + 32)
                    for r in range(2):
                        b = B_BR + 2 * u + r
                        split(b + 2, [(i, 4)])
                        v.tensor_tensor(halves(br_t[:, r]), ring_a(r), halves(g_ab[:, u, r]), ALU.mult
                                        ).then_inc(s_free_a, 1)
                    dve.wait_ge(s_free_a, i * 4 + (A_BR + 2 * u + 2))
                    ch.did(v.tensor_tensor(br_t[:, 2], br_t[:, 0], br_t[:, 1], ALU.add))
                    ch.wait()
                    hi_lo(br_t[:, 2], h_hi[:, i * 2 + u], h_lo[:, i * 2 + u]).then_inc(S["m_done"], 1)
                    dve.wait_ge(S["m_done"], i * 2 + (u + 1))
            dve.wait_ge(S["x_again"], 16)
            with dve.Fori(0, KD // 2) as i:
                for u in range(2):
                    split(B_O + 2 * u + 2, [(i, 4)])
                    split(B_O + 2 * u + 3, [(i, 4)])
                    xt = halves(x[:, i * 2 + u])
                    v.tensor_tensor(xt, xt, ring_a(u), ALU.add).then_inc(s_free_a, 1)
            dve.wait_ge(s_free_a, A_Q)
            norm(1, True)

            def query(t, loops=()):
                bl = [(r, 4) for r in loops]
                split(B_Q + 2 * t + 2, bl)
                split(B_Q + 2 * t + 3, bl)
                if t or loops:
                    dve.wait_ge(S["sc_mm"], at_step(t, [(r, 2) for r in loops]))
                v.tensor_copy(halves(qf[:, t % 2]), ring_a(t)).then_inc(s_free_a, 1)

            def settled():
                ch.wait()
                dve.sem_inc(S["passed"], 1)

            def top16(t, loops=()):
                dve.wait_ge(S["sc_mm"], at_step(t + 2, [(r, 2) for r in loops]))
                ch.did(v.tensor_copy(work[:, 0:4], PS[:, 6, :].rearrange("p (t n) -> p t n", t=4)))
                ch.did(v.tensor_copy(work[0:64, 4], PS[0:64, 7, 0:NK]))
                ch.wait()
                dve.sem_inc(S["sc_f"], 1)
                for k8 in (slice(0, 8), slice(8, 16)):
                    if k8.start:
                        for tt, n in enumerate(ROWS):
                            ch.did(v.match_replace(work[0:n, tt], wv[0:n, tt, 0:8], work[0:n, tt], -3.0e38))
                        settled()
                    for tt, n in enumerate(ROWS):
                        ch.did(v.max(wv[0:n, tt, k8], work[0:n, tt]))
                    settled()
                    for tt, n in enumerate(ROWS):
                        ch.did(v.max_index(wi[0:n, tt, k8], wv[0:n, tt, k8], work[0:n, tt]))
                    settled()
                tile = at_step(t, [(r, 2) for r in loops])
                ch.did(v.tensor_copy(tv[:, 0:4, tile], wv[:, 0:4]))
                ch.did(v.tensor_copy(ti[:, 0:4, tile], wi[:, 0:4]))
                ch.did(v.tensor_copy(tv[0:64, 4, tile], wv[0:64, 4]))
                ch.did(v.tensor_copy(ti[0:64, 4, tile], wi[0:64, 4]))
                ch.wait()

            dve.sem_inc(S["sc_f"], 1)
            query(0)
            with ch.loop(KD // 2 - 1, 2 * (2 + 5 * TT + 4)) as i:
                for u in range(2):
                    query(1 + u, [i])
                    top16(u, [i])
            query(KD - 1)
            top16(KD - 2)
            top16(KD - 1)

            for tt in range(TT):
                n = ROWS[tt]
                ch.wait()
                tvh = tv[0:n, tt].rearrange("p (h s) k -> p h s k", s=2)
                tih = ti[0:n, tt].rearrange("p (h s) k -> p h s k", s=2)
                for s_h in range(PH):
                    ch.did(v.tensor_tensor(comb[0:n, s_h].rearrange("p (a b) -> p a b", a=TOPK),
                                           tvh[:, s_h, 0].unsqueeze(2).broadcast_to([n, TOPK, TOPK]),
                                           tvh[:, s_h, 1].unsqueeze(1).broadcast_to([n, TOPK, TOPK]), ALU.add))
                biv = bi[0:n].rearrange("p (h k) -> p h k", h=PH)
                for half in range(2):
                    k8 = slice(8 * half, 8 * half + 8)
                    ch.wait()
                    for h in range(PH):
                        ch.did(v.max(bv[0:n, tt, h, k8], comb[0:n, h]))
                    ch.wait()
                    for h in range(PH):
                        ch.did(v.max_index(biv[:, h, k8], bv[0:n, tt, h, k8], comb[0:n, h]))
                    if half == 0:
                        ch.wait()
                        for h in range(PH):
                            ch.did(v.match_replace(comb[0:n, h], bv[0:n, tt, h, k8], comb[0:n, h], -3.0e38))
                ch.wait()
                ch.did(v.tensor_copy(gmx[0:n, tt], bv[0:n, tt, :, 0]))
                ch.wait()
                v.tensor_tensor(bv[0:n, tt], bv[0:n, tt], gmx[0:n, tt].unsqueeze(2).broadcast_to([n, PH, TOPK]),
                                ALU.subtract).then_inc(S["ft_x"], 1)
                ch.did(v.tensor_scalar(bab[0:n, 0], bi[0:n], 4, None, ALU.logical_shift_right))
                ch.did(v.tensor_scalar(bab[0:n, 1], bi[0:n], 15, None, ALU.bitwise_and))
                ch.wait()
                ch.did(v.tensor_copy(bf[0:n], bab[0:n]))
                for s in range(2):
                    ch.wait()
                    ch.did(v.tensor_tensor(hot[0:n], bf[0:n, s].unsqueeze(2).broadcast_to([n, P, TOPK]),
                                           iota[0:n, 0:TOPK].unsqueeze(1).broadcast_to([n, P, TOPK]), ALU.is_equal))
                    ch.wait()
                    hot4 = hot[0:n].rearrange("p (h k) a -> p h k a", h=PH)
                    ch.did(v.tensor_tensor(hot4, hot4, tih[:, :, s].unsqueeze(2).broadcast_to([n, PH, TOPK, TOPK]),
                                           ALU.mult))
                    ch.wait()
                    ch.did(v.tensor_reduce(gij[0:n, tt, 1 + s], hot[0:n], AX.X, ALU.add))
            for tt, n in enumerate(ROWS):
                dve.wait_ge(S["ft_e"], tt + 1)
                ch.did(v.tensor_reduce(gmx[0:n, tt], bv[0:n, tt], AX.X, ALU.add))
            ch.wait()
            for tt, n in enumerate(ROWS):
                ch.did(v.reciprocal(gmx[0:n, tt], gmx[0:n, tt]))
            ch.wait()
            for tt, n in enumerate(ROWS):
                v.tensor_tensor(gij[0:n, tt, 0].rearrange("p (h k) -> p h k", h=PH), bv[0:n, tt],
                                gmx[0:n, tt].unsqueeze(2).broadcast_to([n, PH, TOPK]), ALU.mult
                                ).then_inc(S["ft_g"], 1)
            for tt, n in enumerate(ROWS):
                dve.wait_ge(S["tr_g"], tt + 1)
                v.tensor_copy(gij_t[:, tt * P:tt * P + n], PS[:, tt % 4, 0:384].rearrange("p (c t) -> p t c", c=3)[:, 0:n]
                              ).then_inc(S["trf_g"], 1)
            dve.wait_ge(S["trf_g"], TT)

            with ch.loop(NGT // 2, 2 * (1 + 12 * 7)) as i:
                for u in range(2):
                    ch.wait()
                    ch.did(v.tensor_copy(oh_cur[:, u], gij_t[:, bass.ds(i * (2 * GT) + GT * u, GT)]))
                    ch.wait()
                    for n in range(12):
                        dve.wait_ge(S["g_mm"], i * 24 + (12 * u + n + 1))
                        for k in range(4):
                            cur = oh_cur[:, u, 4 * n + k]
                            ch.did(v.tensor_scalar(oh_j[:, n % 2, k], iota[:], cur[:, 2:3], None, ALU.is_equal))
                            last = v.tensor_scalar(oh_i[:, n % 2, k], iota[:], cur[:, 1:2], cur[:, 0:1],
                                                   ALU.is_equal, ALU.mult)
                            if k < 3:
                                ch.did(last)
                            else:
                                last.then_inc(S["oh"], 1)
            dve.wait_ge(S["oh"], T // 4)

            def gated(par, c, g0, loops):
                tl = [(r, GRP * n) for r, n in loops]
                t = GRP * g0 + c
                if c % 2 == 0:
                    dve.wait_ge(S[f"gin{c // 2}"], at_step(16 * (g0 + 1), loops, 16))
                v.tensor_tensor(af[:, c % 2].rearrange("p (a b) -> p a b", a=NGT),
                                gl[:, c % 2].rearrange("p (a b) -> p a b", a=NGT), g_in[:, c // 2, :, c % 2],
                                ALU.mult).then_inc(S["gl"], 1)
                dve.wait_ge(S["gl"], at_step(t + 3, tl))
                hi_lo(af[:, c % 2], a_hi[:, par, c], a_lo[:, par, c]).then_inc(S["a_rdy"], 1)
                dve.wait_ge(S["a_rdy"], at_step(t + 1, tl))

            def from_dram(par, c, g0, loops=()):
                dve.wait_ge(S[f"gl{c % 2}"], at_step(16 * (2 * g0 + c // 2 + 1), loops, 32))
                gated(par, c, g0, loops)

            def chunks(par, b0, g0, loops=()):
                bl, tl = [(r, 16 * n) for r, n in loops], [(r, GRP * n) for r, n in loops]
                for c in range(GRP):
                    t = GRP * g0 + c
                    split(b0 + 2 * c + 2, bl)
                    split(b0 + 2 * c + 3, bl)
                    dve.wait_ge(s_free_b, at_step(N_SPILL + t + 1, tl))
                    gated(par, c, g0, loops)

            def values_beside(g, loops=()):
                bl, tl = [(r, 8 * n) for r, n in loops], [(r, KD * n) for r, n in loops]
                if g or loops:
                    dve.wait_ge(s_free_a, at_step(A_V + KD * g, tl))
                for j in range(4):
                    for s in range(2):
                        dve.wait_ge(S["vt"], at_step(8 * g + 2 * j + s + 1, bl))
                        xt = halves(x[:, 4 * j + 2 * s])
                        v.tensor_tensor(xt, xt, ring_a(0), ALU.add).then_inc(s_free_a, 1)
                        dve.wait_ge(s_used, at_step(B_V + 8 * g + 2 * j + s + 1, bl))
                        xt = halves(x[:, 4 * j + 2 * s + 1])
                        v.tensor_tensor(xt, xt, ring_a(1), ALU.add).then_inc(s_free_a, 1)
                        split(B_V + 8 * g + 2 * j + s + 2, bl)
                        if s == 0:
                            from_dram((g + 1) % 2, j, g + 1, loops)

            def values(b0, g0, loops=()):
                bl, tl = [(r, 16 * n) for r, n in loops], [(r, KD * n) for r, n in loops]
                vl = [(r, 8 * n) for r, n in loops]
                dve.wait_ge(s_free_a, at_step(A_V + KD * g0, tl))
                dve.sem_inc(S["passed"], 1)
                with dve.Fori(0, 4) as j:
                    for s in range(2):
                        dve.wait_ge(S["vt"], at_step(8 * g0 + s + 1, [*vl, (j, 2)]))
                        xt = halves(x[:, j * 4 + 2 * s])
                        v.tensor_tensor(xt, xt, ring_a(0), ALU.add).then_inc(s_free_a, 1)
                        dve.wait_ge(s_used, at_step(b0 + s + 1, [*bl, (j, 2)]))
                        xt = halves(x[:, j * 4 + (2 * s + 1)])
                        v.tensor_tensor(xt, xt, ring_a(1), ALU.add).then_inc(s_free_a, 1)
                        split(b0 + s + 2, [*bl, (j, 2)])

            dve.sem_inc(S["gl"], 2)
            for c in range(GRP):
                from_dram(0, c, 0)
            dve.wait_ge(s_lo, B_V + 2)
            with ch.loop((NPRE - 1) // 2, 2 * GRP) as i:
                for g in range(2):
                    values_beside(g, [(i, 2)])
            values_beside(NPRE - 2)
            with ch.loop((NG - NPRE) // 2, 2 * GRP) as i:
                for g in range(2):
                    chunks((NPRE + g) % 2, B_UV + 16 * g, NPRE + g, [(i, 2)])
                    values(B_UV + 8 + 16 * g, NPRE - 1 + g, [(i, 2)])
            values(B_PG - 8, NG - 1)
            dve.wait_ge(s_free_a, A_PG)

            dve.wait_ge(S["p"], 16)
            for k in range(2):
                hi_lo(p_raw[:, k], p_hi[:, k], p_lo[:, k]).then_inc(S["p_done"], 1)
            for q in range(4):
                for m in range(4):
                    if m < 3:
                        dve.wait_ge(S["vt"], 8 * NG + 3 * q + m + 1)
                    else:
                        dve.wait_ge(s_used, B_PG + q + 1)
                        split(B_PG + q + 2)
                    v.tensor_copy(halves(proj[:, 4 * q + m]), ring_a(m)).then_inc(s_free_a, 1)
            dve.wait_ge(s_free_a, A_PG + KD)
            norm(2, True)
            dve.sem_inc(S["pas"], 2)

            def ple(t, loops=(), more=True):
                bl, tl = [(r, 4) for r in loops], [(r, 2) for r in loops]
                if more:
                    split(B_PG + 4 + 2 * t + 2, bl)
                    split(B_PG + 4 + 2 * t + 3, bl)
                dve.wait_ge(s_free_b, at_step(N_SPILL + NCHUNK + t + 1, tl))
                n = at_step(t, tl)
                ch.did(v.tensor_tensor(proj[:, n], proj[:, n], sg[:, t % 2], ALU.mult))
                ch.wait()
                v.tensor_tensor(x[:, n], x[:, n], proj[:, n], ALU.add).then_inc(S["pas"], 1)

            with ch.loop(KD // 2 - 1, 2) as i:
                for u in range(2):
                    ple(u, [i])
            ple(KD - 2)
            ple(KD - 1, more=False)
            dve.wait_ge(S["pas"], KD + 2)
            norm(3, False)

        @block.tensor
        def _(pe):
            mm = nc.tensor.matmul

            def tile(dst, w, slot_k, xh, xl, ks, first, last, at=0):
                slot, m, kt = slot_k
                wh = whi[:, slot].rearrange("p (m k) c -> p m k c", k=kt)
                wl = wlo[:, slot].rearrange("p (m k) c -> p m k c", k=kt)
                for n, k in enumerate(ks):
                    for r, (w, xx) in enumerate(((wh, xh), (wh, xl), (wl, xh))):
                        for a in range(2):
                            ins = mm(dst[:, a], w[:, m, at + n], xx[:, k, a * TH:(a + 1) * TH],
                                     start=first and n == 0 and r == 0,
                                     stop=last and n == len(ks) - 1 and r == 2)
                return ins

            def full_tile(dst, b, xh, xl, loops=(), h0=None):
                for s in range(2):
                    pe.wait_ge(s_lo, at_step(b + s + 1, loops))
                    if h0 is not None:
                        for k in range(8):
                            pe.wait_ge(S["h_done"], h0 + 8 * s + k + 1)
                            ins = tile(dst, None, ((b + s) % 2, 0, 8), xh, xl, [8 * s + k], s + k == 0,
                                       s * k == 7, at=k)
                        ins.then_inc(s_used, 1)
                        continue
                    tile(dst, None, ((b + s) % 2, 0, 8), xh, xl, range(8 * s, 8 * s + 8), s == 0, s == 1
                         ).then_inc(s_used, 1)

            def norm(r):
                for k in range(KD):
                    pe.wait_ge(S["sq"], KD * r + k + 1)
                    for a in range(2):
                        ins = mm(PS[:, 4 + a, 0:TH], ones[:], sq[:, k % 2, a * TH:(a + 1) * TH],
                                 start=k == 0, stop=k == KD - 1)
                    ins.then_inc(S["sqm"], 1)

            pe.wait_ge(S["ones"], 16)
            pe.sem_inc(S["sqm"], 2)
            norm(0)
            pe.wait_ge(S["const"], 144)

            def project(ring, s_free, f0, h0, b0, n):
                for t in range(2):
                    if f0:
                        pe.wait_ge(s_free, f0 + t - 1)
                    full_tile(ring(t), b0 + 2 * t, h_hi, h_lo, h0=None if t else h0)
                with pe.Fori(1, n // 2) as i:
                    for u in range(2):
                        pe.wait_ge(s_free, i * 2 + (f0 + u - 1))
                        full_tile(ring(u), b0 + 2 * u, h_hi, h_lo, [(i, 4)])

            project(ring_a, s_free_a, 0, 0, B_IN, N_FEAT)
            project(ring_b, s_free_b, 0, None, B_IN + 2 * N_FEAT, N_SPILL)

            ROPE = list(range(QA, KA + 2)) + list(range(QR, KR + 4))
            pe.wait_ge(s_free_a, A_BR)
            pe.wait_ge(s_free_b, N_SPILL)
            for r, f in enumerate(ROPE):
                if r >= 2:
                    pe.wait_ge(S["rotf"], r - 1)
                for a in range(2):
                    ins = mm(PS[:, 2 * (r % 2) + a, 0:TH], swap[:], feat[:, f, a * TH:(a + 1) * TH],
                             start=True, stop=True)
                ins.then_inc(S["rot"], 1)
            for tt in range(TT):
                n = ROWS[tt]
                c = slice(tt * P, tt * P + n)
                if tt:
                    pe.wait_ge(S["trf_a"], tt)
                for f in range(2):
                    ins = pe.transpose(PS[0:n, 4, f * P:(f + 1) * P], feat[:, VA + f, c], ident[:])
                ins.then_inc(S["tr_a"], 1)
                if tt:
                    pe.wait_ge(S["trf_v"], tt)
                for f in range(8):
                    ins = pe.transpose(PS[0:n, 6 + f // 4, (f % 4) * P:(f % 4 + 1) * P], feat[:, VR + f, c], ident[:])
                ins.then_inc(S["tr_v"], 1)
                if tt:
                    pe.wait_ge(S["trf_k"], tt)
                else:
                    pe.wait_ge(S["rope"], len(ROPE))
                for f in range(4):
                    ins = pe.transpose(PS[0:n, 5, f * P:(f + 1) * P], feat[:, KR + f, c], ident[:])
                ins.then_inc(S["tr_k"], 1)

            def a_scores(n):
                t, c = n // 4, n % 4
                if n >= 2:
                    pe.wait_ge(S["as_m"], n - 1)
                k0 = max(c - 1, 0) * P
                w = (c + 1) * P - k0
                for u in range(2):
                    r = slice(64 * u, 64 * u + 64)
                    ins = mm(PS[:, 2 * (n % 2) + u, 0:w], feat[r, QA + t, c * P:(c + 1) * P],
                             feat[r, KA + t // 4, k0:(c + 1) * P], start=True, stop=True)
                ins.then_inc(S["as_mm"], 1)

            def a_turn(n):
                pe.wait_ge(S["as_p"], n + 1)
                if n >= 2:
                    pe.wait_ge(S["as_tc"], n - 1)
                else:
                    pe.wait_ge(S["trf_a"], TT)
                    pe.wait_ge(S["trf_k"], TT)
                nb = 1 if n % 4 == 0 else 2
                for u in range(2):
                    for k in range(nb):
                        j = u * nb + k
                        ins = pe.transpose(PS[:, 4 + n % 2, j * P:(j + 1) * P], sm[:, n % 2, u, k * P:(k + 1) * P],
                                           ident[:])
                ins.then_inc(S["as_t"], 1)

            def a_values(n):
                t, c = n // 4, n % 4
                pe.wait_ge(S["as_tc"], n + 1)
                if n >= 2:
                    pe.wait_ge(S["as_of"], n - 1)
                else:
                    pe.wait_ge(S["trf_v"], TT)
                nb = 1 if c == 0 else 2
                for u in range(2):
                    kv = 2 * (t // 4) + u
                    for k in range(nb):
                        ins = mm(PS[64 * u:64 * u + 64, 6 + n % 2, 0:P],
                                 v_tok[:, c - nb + 1 + k, kv * DA:(kv + 1) * DA], pT[:, n % 2, u * nb + k],
                                 start=k == 0, stop=k == nb - 1)
                ins.then_inc(S["as_o"], 1)

            a_scores(0)
            for n in range(32 + 2):
                if n + 1 < 32:
                    a_scores(n + 1)
                if 1 <= n < 33:
                    a_turn(n - 1)
                if n >= 2:
                    a_values(n - 2)

            def b_scores(b):
                if b >= 2:
                    pe.wait_ge(S["bs_m"], b - 1)
                else:
                    pe.wait_ge(S["as_m"], 32)
                for kv in range(KVA):
                    p, u = kv // 2, kv % 2
                    r = slice(64 * u, 64 * u + 64)
                    q = qs[r, b, p]
                    rows = slice(32 * kv, 32 * kv + 32)
                    bank = 2 * (b % 2) + u
                    mm(PS[rows, bank, 0:P], q, ck[r, b, p], start=True, stop=True)
                    ins = mm(PS[rows, bank, P:P + 64], q, feat[r, KA + p, NP_TOK:T], start=True, stop=True)
                ins.then_inc(S["bs_mm"], 1)

            def b_turn(b):
                pe.wait_ge(S["bs_p"], b + 1)
                if b >= 2:
                    pe.wait_ge(S["bs_tc"], 2 * b - 2)
                else:
                    pe.wait_ge(S["as_tc"], 32)
                pe.transpose(PS[:, 4 + b % 2, 0:P], sm[:, b % 2, 0, 0:P], ident[:])
                pe.transpose(PS[0:64, 4 + b % 2, P:2 * P], sm[:, b % 2, 0, P:P + 64], ident[:]
                             ).then_inc(S["bs_t"], 1)

            def b_values(b):
                pe.wait_ge(S["bs_tc"], 2 * b + 2)
                if b >= 2:
                    pe.wait_ge(S["bs_of"], b - 1)
                else:
                    pe.wait_ge(S["as_of"], 32)
                for kv in range(KVA):
                    p, u = kv // 2, kv % 2
                    dst = PS[64 * u:64 * u + 64, 6 + b % 2, 32 * p:32 * p + 32]
                    c = slice(kv * DA, (kv + 1) * DA)
                    r = slice(32 * kv, 32 * kv + 32)
                    mm(dst, cv[:, b, c], pT[:, b % 2, 0, r], start=True, stop=False)
                    ins = mm(dst, v_tok[0:64, 4, c], pT[0:64, b % 2, 1, r], start=False, stop=True)
                ins.then_inc(S["bs_o"], 1)

            for u in range(2):
                pe.wait_ge(S[f"kv{u}"], 16)
            b_scores(0)
            for b in range(NB_S + 2):
                if b + 1 < NB_S:
                    b_scores(b + 1)
                if 1 <= b < NB_S + 1:
                    b_turn(b - 1)
                if b >= 2:
                    b_values(b - 2)

            pe.wait_ge(S["bs_m"], NB_S)
            pe.wait_ge(S["bs_tc"], 2 * NB_S)
            pe.wait_ge(S["bs_of"], NB_S)
            for n in range(16):
                c, t = n // 4, n % 4
                cols = slice(c * P, (c + 1) * P)
                if n:
                    pe.wait_ge(S["rt_at"], n)
                for u in range(2):
                    r = slice(64 * u, 64 * u + 64)
                    ins = mm(PS[:, u, 0:P], feat[r, KR + t, cols], feat[r, QR + t, cols], start=True, stop=True)
                ins.then_inc(S["rt_mm"], 1)
                if c:
                    pe.wait_ge(S["rt_qx"], n + 1)
                    pe.wait_ge(S["rt_sf"], n - 3)
                    if n > 4:
                        pe.wait_ge(S["rt_of"], n - 4)
                    for u in range(2):
                        r = slice(64 * u, 64 * u + 64)
                        mm(PS[:, 4 + u, 0:P], s_prompt[r, t], qx[r, n % 2], start=True, stop=True)
                if n:
                    pe.wait_ge(S["rt_sf"], n)
                for u in range(2):
                    h = 2 * t + u
                    ins = mm(PS[64 * u:64 * u + 64, 6, 0:P], k_tok[:, c, h], vr_tok[:, c, h], start=True, stop=True)
                ins.then_inc(S["rt_s"], 1)
                pe.wait_ge(S["rt_at"], n + 1)
                if n:
                    pe.wait_ge(S["ro_c"], n)
                for u in range(2):
                    ins = mm(PS[:, 2 + u, 0:P], vr_tok[:, c, 2 * t + u], att[:, n % 2, u], start=True, stop=True)
                ins.then_inc(S["rt_o"], 1)
            pe.wait_ge(S["rt_of"], 12)
            for t in range(4):
                pe.wait_ge(S["st_at"] if t else S["rt_at"], t if t else 16)
                for u in range(2):
                    r = slice(64 * u, 64 * u + 64)
                    ins = mm(PS[0:64, u, 0:64], feat[r, KR + t, NP_TOK:T], feat[r, QR + t, NP_TOK:T],
                             start=True, stop=True)
                ins.then_inc(S["st_mm"], 1)
                pe.wait_ge(S["rt_qx"], 16 + t + 1)
                pe.wait_ge(S["s0"], 64)
                if t:
                    pe.wait_ge(S["st_of"], t)
                for u in range(2):
                    r = slice(64 * u, 64 * u + 64)
                    for b in range(NB_S):
                        mm(PS[:, 4 + u, 8 * b:8 * b + 8], s0[t][r, b], qx[r, t % 2, 8 * b:8 * b + 8],
                           start=True, stop=True)
                pe.wait_ge(S["st_kb"], 2 * t + 2)
                if t:
                    pe.wait_ge(S["st_sf"], 2 * t)
                else:
                    pe.wait_ge(S["rt_sf"], 16)
                for q in range(2):
                    for u in range(2):
                        for b in range(4):
                            ins = mm(PS[64 * u:64 * u + 64, 6 + q, b * P:(b + 1) * P], kb[0:64, u, 4 * q + b],
                                     vr_tok[0:64, 4, 2 * t + u], start=True, stop=True)
                    ins.then_inc(S["st_s"], 1)
                pe.wait_ge(S["st_at"], t + 1)
                pe.wait_ge(S["ro_c"], 16 + t)
                for u in range(2):
                    ins = mm(PS[:, 2 + u, 0:64], vr_tok[0:64, 4, 2 * t + u], att[0:64, t % 2, u, 0:64],
                             start=True, stop=True)
                ins.then_inc(S["st_o"], 1)

            pe.wait_ge(S["ro_c"], 20)
            pe.wait_ge(S["st_of"], 4)
            pe.wait_ge(S["st_at"], 4)
            pe.wait_ge(S["st_sf"], 8)
            for h in range(HR + 1):
                if h < HR:
                    if h >= 2:
                        pe.wait_ge(S["gn_dd"], h - 1)
                    for a in range(2):
                        ins = mm(PS[:, 4 * (h % 2) + a, 0:TH], ones[:], o_r[:, h, a * TH:(a + 1) * TH],
                                 start=True, stop=True)
                    ins.then_inc(S["gn_mu"], 1)
                if h >= 1:
                    pe.wait_ge(S["gn_q"], h)
                    if h >= 3:
                        pe.wait_ge(S["gn_vv"], h - 2)
                    for a in range(2):
                        ins = mm(PS[:, 4 * ((h - 1) % 2) + 2 + a, 0:TH], ones[:], gn_sq[:, a * TH:(a + 1) * TH],
                                 start=True, stop=True)
                    ins.then_inc(S["gn_v"], 1)

            pe.wait_ge(S["oab"], 8)
            pe.wait_ge(S["gn_done"], HR)
            for m in range(2):
                for r, (xh, xl) in enumerate(((oa_hi, oa_lo), (or_hi, or_lo))):
                    b = B_BR + 2 * m + r
                    pe.wait_ge(s_free_a, A_BR + 2 * m + r - 1)
                    pe.wait_ge(s_lo, b + 1)
                    tile(ring_a(r), None, (r, 0, 8), xh, xl, range(8), True, True).then_inc(s_used, 1)
            with pe.Fori(2, KD) as m:
                for r, (xh, xl) in enumerate(((oa_hi, oa_lo), (or_hi, or_lo))):
                    pe.wait_ge(s_free_a, m * 2 + (A_BR + r - 1))
                    pe.wait_ge(s_lo, m * 2 + (B_BR + r + 1))
                    tile(ring_a(r), None, (r, 0, 8), xh, xl, range(8), True, True).then_inc(s_used, 1)
            pe.wait_ge(S["m_done"], KD)
            project(ring_a, s_free_a, A_O, None, B_O, KD)
            norm(1)

            def query(t, loops=()):
                pe.wait_ge(s_free_a, at_step(A_Q + t - 1, [(r, 2) for r in loops]))
                full_tile(ring_a(t), B_Q + 2 * t, h_hi, h_lo, [(r, 4) for r in loops],
                          None if t or loops else KD)

            def scores(t, loops=()):
                l2 = [(r, 2) for r in loops]
                pe.wait_ge(s_free_a, at_step(A_Q + t + 1, l2))
                pe.wait_ge(S["sc_f"], at_step(t + 1, l2))
                for tt, n in enumerate(ROWS):
                    ins = mm(PS[0:n, 6 + tt // 4, (tt % 4) * NK:(tt % 4 + 1) * NK], qf[:, t % 2, tt * P:tt * P + n],
                             sub_k[:, t % 2], start=True, stop=True)
                ins.then_inc(S["sc_mm"], 1)

            pe.sem_inc(S["sc_mm"], 1)
            query(0)
            with pe.Fori(0, KD // 2 - 1) as i:
                for u in range(2):
                    query(1 + u, [i])
                    scores(u, [i])
            query(KD - 1)
            scores(KD - 2)
            scores(KD - 1)

            def plain(t, loops=()):
                pe.wait_ge(s_free_b, at_step(N_SPILL + t - 1, [(r, 2) for r in loops]))
                full_tile(ring_b(t), B_U + 2 * t, h_hi, h_lo, [(r, 4) for r in loops])

            plain(0)
            pe.wait_ge(S["sc_f"], KD + 1)
            plain(1)
            with pe.Fori(0, PRE_A // 2 - 1) as i:
                for u in range(2):
                    plain(2 + u, [i])
            pe.wait_ge(s_free_a, A_V)
            for tt, n in enumerate(ROWS):
                pe.wait_ge(S["ft_g"], tt + 1)
                if tt >= 4:
                    pe.wait_ge(S["trf_g"], tt - 3)
                for c in range(3):
                    ins = pe.transpose(PS[:, tt % 4, c * P:c * P + n], gij[0:n, tt, c], ident[0:n, 0:n])
                ins.then_inc(S["tr_g"], 1)
            pe.sem_inc(S["g_mm"], 2)
            with pe.Fori(0, NGT // 2) as i:
                for c in range(2):
                    t, n = PRE_A + c, 12 * c
                    pe.wait_ge(s_free_b, i * 2 + (N_SPILL + t - 1))
                    for s in range(2):
                        pe.wait_ge(s_lo, i * 4 + (B_U + 2 * t + s + 1))
                        for k in range(8):
                            ins = tile(ring_b(t), None, (s, 0, 8), h_hi, h_lo, [8 * s + k], s + k == 0, s * k == 7,
                                       at=k)
                            if k == 7:
                                ins.then_inc(s_used, 1)
                            if k in (2, 5):
                                continue
                            pe.wait_ge(S["oh"], i * 24 + (n + 1))
                            pe.wait_ge(S["g_ev"], i * 24 + (n + 1))
                            for q in range(4):
                                ins = mm(PS[:, n % 2, q * P:(q + 1) * P], oh_j[:, n % 2, q], oh_i[:, n % 2, q],
                                         start=True, stop=True)
                            ins.then_inc(S["g_mm"], 1)
                            n += 1
            with pe.Fori(0, (PRE - PRE_B) // 2) as i:
                for u in range(2):
                    plain(PRE_B + u, [i])
            pe.wait_ge(S["g_ev"], T // 4 + 2)

            def chunks(b0, g0, loops=()):
                bl, tl = [(r, 16 * n) for r, n in loops], [(r, GRP * n) for r, n in loops]
                with pe.Fori(0, GRP // 2) as j:
                    for u in range(2):
                        pe.wait_ge(s_free_b, at_step(N_SPILL + GRP * g0 + u - 1, [*tl, (j, 2)]))
                        full_tile(ring_b(u), b0 + 2 * u, h_hi, h_lo, [*bl, (j, 4)])

            def values(par, b0, g0, loops=(), per=16):
                bl, tl = [(r, per * n) for r, n in loops], [(r, KD * n) for r, n in loops]
                pe.wait_ge(S["a_rdy"], at_step(GRP * (g0 + 1), [(r, GRP * n) for r, n in loops]))
                pe.sem_inc(S["passed_pe"], 1)
                with pe.Fori(0, 4) as j:
                    for s in range(2):
                        pe.wait_ge(s_lo, at_step(b0 + s + 1, [*bl, (j, 2)]))
                        for m in range(2):
                            pe.wait_ge(s_free_a, at_step(A_V + KD * g0 + 2 * s + m - 1, [*tl, (j, 4)]))
                            tile(ring_a(m), None, (s, m, GRP), a_hi[:, par], a_lo[:, par], range(GRP), True, True
                                 ).then_inc(S["vt"] if m == 0 else s_used, 1)

            with pe.Fori(0, (NPRE - 1) // 2) as i:
                for g in range(2):
                    values(g, B_V + 8 * g, g, [(i, 2)], per=8)
            values(NPRE % 2, B_V + 8 * (NPRE - 2), NPRE - 2)
            with pe.Fori(0, (NG - NPRE) // 2) as i:
                for g in range(2):
                    chunks(B_UV + 16 * g, NPRE + g, [(i, 2)])
                    values((NPRE - 1 + g) % 2, B_UV + 8 + 16 * g, NPRE - 1 + g, [(i, 2)])
            values(1, B_PG - 8, NG - 1)

            pe.wait_ge(S["p_done"], 2)
            for q in range(4):
                pe.wait_ge(s_lo, B_PG + q + 1)
                for m in range(4):
                    pe.wait_ge(s_free_a, A_PG + 4 * q + m - 1)
                    tile(ring_a(m), None, (q % 2, m, 2), p_hi, p_lo, range(2), True, True
                         ).then_inc(S["vt"] if m < 3 else s_used, 1)
            norm(2)
            project(ring_b, s_free_b, N_SPILL + NCHUNK, 2 * KD, B_PG + 4, KD)
            norm(3)


def _tables():
    f = np.float32
    t = {}
    t["ones"] = np.ones((P, P), f)
    t["ident"] = np.eye(P, dtype=f)
    sw = np.zeros((P, P), f)
    for p in range(P):
        if p % 64 < 32:
            sw[p + 32, p] = -1.0
        else:
            sw[p - 32, p] = 1.0
    t["swap"] = sw
    t["iota"] = np.tile(np.arange(P, dtype=f), (P, 1))
    inv = (10000.0 ** (-np.arange(0, DA, 2) / DA)).astype(f)
    pos = np.concatenate([np.arange(NP_TOK), PAST + np.tile(np.arange(NS_S), NB_S)]).astype(f)
    ang = (pos[None, :] * inv[:, None]).astype(f)
    t["cos"] = np.tile(np.cos(ang), (4, 1)).astype(f)
    t["sin"] = np.tile(np.sin(ang), (4, 1)).astype(f)
    i, k = np.arange(P)[:, None], np.arange(256)[None, :]
    t["mask_p"] = np.where((k >= i) & (k <= i + P), 0.0, -1e30).astype(f)
    s = np.arange(P)[:, None] % NS_S
    t["mask_c"] = np.where(np.arange(P)[None, :] >= s, 0.0, -1e30).astype(f)
    j = np.arange(64)[None, None, :]
    b = np.arange(NB_S)[None, :, None]
    t["mask_n"] = np.where((j // NS_S == b) & (j % NS_S <= s[:, :, None]), 0.0, -1e30).astype(f)
    lg = np.log1p(-np.exp2(-5.0 - np.arange(HR, dtype=f))).astype(f)
    jj, ii = np.arange(P)[:, None, None], np.arange(P)[None, None, :]
    t["intra"] = np.where(ii >= jj, np.exp(np.maximum(ii - jj, 0).astype(f) * lg[None, :, None]), 0).astype(f)
    jj, ii = np.arange(64)[:, None, None], np.arange(64)[None, None, :]
    same = (jj // 8 == ii // 8) & (ii >= jj)
    t["intra_s"] = np.zeros((P, HR, 64), f)
    t["intra_s"][:64] = np.where(same, np.exp(np.maximum(ii - jj, 0).astype(f) * lg[None, :, None]), 0)
    head = 2 * np.arange(4)[None, :] + np.arange(P)[:, None] // 64
    step = np.concatenate([np.arange(P), np.tile(np.arange(NS_S), NB_S)]).astype(f) + f(1)
    t["cross"] = np.exp(step[None, None, :] * lg[head][:, :, None]).astype(f)
    t["kdec"] = np.exp((P - 1 - np.arange(P, dtype=f))[:, None] * lg[None, :]).astype(f)
    t["mkd"] = np.zeros((P, HR, NB_S), f)
    r = np.arange(64)
    t["mkd"][:64] = np.where((r // 8)[:, None, None] == np.arange(NB_S)[None, None, :],
                             np.exp((NS_S - 1 - r % 8).astype(f)[:, None] * lg[None, :])[:, :, None], 0)
    t["cdec"] = np.stack([np.exp(f(P) * lg[head]), np.exp(f(NS_S) * lg[head])], 1).astype(f)
    return t


def _lay(w, kt, mt):
    K, M = w.shape
    a = w.reshape(K // (P * kt), kt, P, M // (P * mt), mt, P)
    return a.transpose(3, 0, 2, 4, 1, 5).reshape(-1, P, mt * kt * P)


def kernel(**inputs):
    import concourse.bacc as _bacc
    from concourse.bass_utils import run_bass_kernel_spmd as _run

    g = {n: np.asarray(a) for n, a in inputs.items()}
    f = np.float32
    heads = [(2 * (t // 4) + u) * 4 + t % 4 for t in range(8) for u in range(2)]
    w_in = g["w_in"][0]
    qa = w_in[:, :HA * DA].reshape(D, HA, DA)[:, heads].reshape(D, HA * DA)
    w_a = g["w_branch_attn"][0].reshape(HA, DA, D)[heads].reshape(HA * DA, D)
    br = np.stack([_lay(w_a, 8, 1), _lay(g["w_branch_ret"][0], 8, 1)], 1).reshape(-1, P, 8 * P)
    u_t = g["peer_u"][0].T
    ub = _lay(u_t, 8, 1).reshape(NG, 8, P, 8 * P)
    vb = np.stack([_lay(g["peer_v"][0][n * 512:(n + 1) * 512], 4, 2) for n in range(NG)])
    uv = [*ub[:NPRE], *vb[:NPRE - 1]]
    for n in range(NPRE - 1, NG - 1):
        uv += [ub[n + 1], vb[n]]
    uv.append(vb[NG - 1])
    w = np.concatenate([_lay(qa, 8, 1), _lay(w_in[:, HA * DA:], 8, 1), br, _lay(g["w_out"][0], 8, 1),
                        _lay(g["w_peer_query"][0], 8, 1), *uv, _lay(g["w_ple_proj"][0], 2, 4),
                        _lay(g["w_ple_gate"][0], 8, 1)])

    def feature_major(a, b, k):
        both = np.concatenate([a.reshape(-1, k * P), b.reshape(-1, k * P)])
        return both.T.reshape(k, P, T).transpose(1, 0, 2)

    sinks = g["attn_sinks"][0]
    arrays = dict(
        w=w, xT=feature_major(g["x_prompt"], g["x_sample"], KD), pT=feature_major(g["p_prompt"], g["p_sample"], 2),
        lns=np.stack([a.reshape(KD, P).T for a in (g["ln1"][0], g["ln2"][0], g["ln_ple"][0], g["ln_final"])], 1),
        ln_ret=g["ln_ret"][0].reshape(HR, P).T,
        sink_q=np.tile(sinks[heads].reshape(1, 8, 2), (P, 1, 1)), sink_r=np.repeat(sinks, 8)[:, None],
        sub_k=g["peer_sub_keys"][0].transpose(2, 0, 1),
        ckT=g["cache_k_win"][0].reshape(NB_S, P, 2, 2, DA).transpose(3, 4, 0, 2, 1).reshape(P, NB_S, 2, P),
        cache_k=g["cache_k_win"][0].reshape(NB_S, P, 256), cache_v=g["cache_v_win"][0].reshape(NB_S, P, 256),
        state=g["state_ret"][0].reshape(NB_S, 4, 2, DKR, DVR).transpose(2, 3, 1, 0, 4).reshape(P, 4, NB_S, DVR),
        **_tables())
    outs = dict(y=(P, KD, T), kc=(NB_S, P - NS_S, 256), vc=(NB_S, P - NS_S, 256), k_new=(P, 2, 192),
                v_new=(P, 2, 192), s_pr=(P, 4, DVR), s_smp=(P, 4, NB_S, DVR))
    nc = _bacc.Bacc("TRN2", target_bir_lowering=False, num_devices=1)
    d, o = {}, {}
    arrays = {n: np.ascontiguousarray(a) for n, a in arrays.items()}
    for n, a in arrays.items():
        d[n] = nc.dram_tensor("in_" + n, a.shape, mybir.dt.from_np(a.dtype), kind="ExternalInput").ap()
    for n, s in outs.items():
        o[n] = nc.dram_tensor("out_" + n, s, F32, kind="ExternalOutput").ap()
    d["spill"] = nc.dram_tensor("spill_scr", (N_SPILL, P, T), F32, kind="Internal").ap()
    d["asp"] = nc.dram_tensor("act_scr", (PRE, P, T), F32, kind="Internal").ap()
    d["g_scr"] = nc.dram_tensor("gate_scr", (NGT, P, NK, GT), F32, kind="Internal").ap()
    build(nc, d, o)
    r = _run(nc, [{"in_" + n: a for n, a in arrays.items()}], core_ids=[0]).results[0]
    r = {n: np.asarray(r["out_" + n]) for n in outs}

    y = r["y"].transpose(2, 1, 0).reshape(T, D)

    def window(a):
        return a.reshape(2, DA, 2, -1).transpose(3, 2, 0, 1).reshape(-1, KVA, DA)

    kn, vn = window(r["k_new"]), window(r["v_new"])
    k_p, v_p = kn[None, None, :P], vn[None, None, :P]
    k_s, v_s = (np.concatenate([c.reshape(NB_S, P - NS_S, KVA, DA), n[P:].reshape(NB_S, NS_S, KVA, DA)], 1)[None]
                for c, n in ((r["kc"], kn), (r["vc"], vn)))
    s_p = r["s_pr"].reshape(2, DKR, 4, DVR).transpose(2, 0, 1, 3).reshape(1, 1, HR, DKR, DVR)
    s_s = r["s_smp"].reshape(2, DKR, 4, NB_S, DVR).transpose(3, 2, 0, 1, 4).reshape(1, NB_S, HR, DKR, DVR)
    return (y[:NP_TOK].reshape(1, NP_TOK, D), y[NP_TOK:].reshape(NB_S, NS_S, D), k_p, v_p, s_p, k_s, v_s, s_s)
```
